# Optimizing a Trainium2 kernel written in Bass

```python
import math
import jax, jax.numpy as jnp
from jax import lax
import numpy as np

D_MODEL = 2048
BATCH = 1
SEQ = 256
DEPTH = 1

HEAD_DIM = 128
MOBA_HEADS = D_MODEL // (2 * HEAD_DIM)
MOBA_BLOCK = 256
MOBA_TOPK = 3
MOBA_Q_CHUNK = 64
DIFF_HEADS = D_MODEL // (4 * HEAD_DIM)
DIFF_V_DIM = 2 * HEAD_DIM
DIFF_Q_BLOCK = 128
ROT_DIM = HEAD_DIM // 4
ROPE_THETA = 500000.0
D_FF = 4 * D_MODEL
PLE_DIM = 256
NORM_EPS = 1e-6
MOBA_WIDTH = MOBA_HEADS * HEAD_DIM
DIFF_QK_WIDTH = DIFF_HEADS * 2 * HEAD_DIM
DIFF_V_WIDTH = DIFF_HEADS * DIFF_V_DIM
IN_WIDTH = 3 * MOBA_WIDTH + 2 * DIFF_QK_WIDTH + DIFF_V_WIDTH + 2 * D_MODEL


F32 = jnp.float32

def rmsnorm(x, g):
    xf = x.astype(F32)
    y = xf * lax.rsqrt(jnp.mean(xf * xf, axis=-1, keepdims=True) + NORM_EPS)
    return (y * g.astype(F32)).astype(x.dtype)

def partial_rope(x, pos_f):
    half = ROT_DIM // 2
    inv_freq = 1.0 / (ROPE_THETA ** (jnp.arange(half, dtype=F32) * 2.0 / ROT_DIM))
    ang = pos_f[:, None] * inv_freq[None, :]
    cos, sin = jnp.cos(ang), jnp.sin(ang)
    xf = x.astype(F32)
    x1 = xf[..., :half]
    x2 = xf[..., half:ROT_DIM]
    out = jnp.concatenate([x1 * cos - x2 * sin, x2 * cos + x1 * sin, xf[..., ROT_DIM:]], axis=-1)
    return out.astype(x.dtype)

def moba_attention(q, k, v):
    B, H, S, Dh = q.shape
    nb = -(-S // MOBA_BLOCK)
    topk = min(MOBA_TOPK, nb)
    pad = nb * MOBA_BLOCK - S
    k_p = jnp.pad(k, ((0, 0), (0, 0), (0, pad), (0, 0)))
    v_p = jnp.pad(v, ((0, 0), (0, 0), (0, pad), (0, 0)))
    k_blk = k_p.reshape(B, H, nb, MOBA_BLOCK, Dh)
    v_blk = v_p.reshape(B, H, nb, MOBA_BLOCK, Dh)
    k_mean = jnp.mean(k_blk.astype(F32), axis=3)
    nc = S // MOBA_Q_CHUNK
    q_ch = jnp.moveaxis(q.reshape(B, H, nc, MOBA_Q_CHUNK, Dh), 2, 0)
    bi = jnp.arange(B)[:, None, None, None]
    hi = jnp.arange(H)[None, :, None, None]
    blk_ids = jnp.arange(nb)
    scale = Dh ** -0.5

    def chunk(args):
        ci, qc = args
        q_start = ci * MOBA_Q_CHUNK
        cur = q_start // MOBA_BLOCK
        gate = jnp.einsum('bhqd,bhnd->bhqn', qc.astype(F32), k_mean)
        gate = jnp.where(blk_ids < cur, gate, -jnp.inf)
        _, idx = lax.top_k(gate, topk)
        valid = idx < cur
        k_sel = k_blk[bi, hi, idx]
        v_sel = v_blk[bi, hi, idx]
        s_sel = jnp.einsum('bhqd,bhqjkd->bhqjk', qc, k_sel).astype(F32) * scale
        s_sel = jnp.where(valid[..., None], s_sel, -jnp.inf)
        s_sel = s_sel.reshape(B, H, MOBA_Q_CHUNK, topk * MOBA_BLOCK)
        own0 = cur * MOBA_BLOCK
        k_own = lax.dynamic_slice_in_dim(k_p, own0, MOBA_BLOCK, axis=2)
        v_own = lax.dynamic_slice_in_dim(v_p, own0, MOBA_BLOCK, axis=2)
        s_own = jnp.einsum('bhqd,bhkd->bhqk', qc, k_own).astype(F32) * scale
        q_pos = q_start + jnp.arange(MOBA_Q_CHUNK)
        k_pos = own0 + jnp.arange(MOBA_BLOCK)
        s_own = jnp.where(k_pos[None, :] <= q_pos[:, None], s_own, -jnp.inf)
        probs = jax.nn.softmax(jnp.concatenate([s_sel, s_own], axis=-1), axis=-1).astype(v.dtype)
        p_sel = probs[..., :topk * MOBA_BLOCK].reshape(B, H, MOBA_Q_CHUNK, topk, MOBA_BLOCK)
        p_own = probs[..., topk * MOBA_BLOCK:]
        return (jnp.einsum('bhqjk,bhqjkd->bhqd', p_sel, v_sel)
                + jnp.einsum('bhqk,bhkd->bhqd', p_own, v_own))

    out = lax.map(chunk, (jnp.arange(nc), q_ch))
    return jnp.moveaxis(out, 0, 2).reshape(B, H, S, Dh)

def diff_attention(q, k, v, lam, sub_g, lambda_init):
    B, H, _, S, Dh = q.shape
    nq = S // DIFF_Q_BLOCK
    q_bl = jnp.moveaxis(q.reshape(B, H, 2, nq, DIFF_Q_BLOCK, Dh), 3, 0)
    k_pos = jnp.arange(S)
    scale = Dh ** -0.5

    def block(args):
        bidx, qb = args
        s = jnp.einsum('bhcqd,bhckd->bhcqk', qb, k).astype(F32) * scale
        q_pos = bidx * DIFF_Q_BLOCK + jnp.arange(DIFF_Q_BLOCK)
        s = jnp.where(k_pos[None, :] <= q_pos[:, None], s, -jnp.inf)
        pr = jax.nn.softmax(s, axis=-1)
        attn = (pr[:, :, 0] - lam * pr[:, :, 1]).astype(v.dtype)
        return jnp.einsum('bhqk,bhkd->bhqd', attn, v)

    out = lax.map(block, (jnp.arange(nq), q_bl))
    out = jnp.moveaxis(out, 0, 2).reshape(B, H, S, DIFF_V_DIM)
    return (rmsnorm(out, sub_g) * (1.0 - lambda_init)).astype(v.dtype)

def first_inputs(seed: int = 0) -> dict:
    key = jax.random.key(seed)
    ks = jax.random.split(key, 24)
    n = lambda k_, shape, s: jax.random.normal(k_, shape, F32) * s
    gain = lambda k_, dim: 1.0 + 0.02 * jax.random.normal(k_, (DEPTH, dim), F32)
    return {
        "x": n(ks[0], (BATCH, SEQ, D_MODEL), 1.0),
        "p": n(ks[1], (DEPTH, BATCH, SEQ, PLE_DIM), 1.0),
        "w_in": n(ks[2], (DEPTH, D_MODEL, IN_WIDTH), D_MODEL ** -0.5),
        "w_br_moba": n(ks[3], (DEPTH, MOBA_WIDTH, D_MODEL), MOBA_WIDTH ** -0.5),
        "w_br_diff": n(ks[4], (DEPTH, DIFF_V_WIDTH, D_MODEL), DIFF_V_WIDTH ** -0.5),
        "w_out": n(ks[5], (DEPTH, D_MODEL, D_MODEL), D_MODEL ** -0.5),
        "lambda_q1": n(ks[6], (DEPTH, HEAD_DIM), 0.1),
        "lambda_k1": n(ks[7], (DEPTH, HEAD_DIM), 0.1),
        "lambda_q2": n(ks[8], (DEPTH, HEAD_DIM), 0.1),
        "lambda_k2": n(ks[9], (DEPTH, HEAD_DIM), 0.1),
        "diff_subln_g": gain(ks[10], DIFF_V_DIM),
        "g_mix_pre": gain(ks[11], D_MODEL),
        "g_mix_post": gain(ks[12], D_MODEL),
        "w_up": n(ks[13], (DEPTH, D_MODEL, D_FF), D_MODEL ** -0.5),
        "w_down": n(ks[14], (DEPTH, D_FF, D_MODEL), D_FF ** -0.5),
        "g_mlp_pre": gain(ks[15], D_MODEL),
        "g_mlp_post": gain(ks[16], D_MODEL),
        "w_ple_proj": n(ks[17], (DEPTH, PLE_DIM, D_MODEL), PLE_DIM ** -0.5),
        "w_ple_gate": n(ks[18], (DEPTH, D_MODEL, D_MODEL), D_MODEL ** -0.5),
        "g_ple_pre": gain(ks[19], D_MODEL),
        "g_ple_post": gain(ks[20], D_MODEL),
    }

def first_block(x, p, w_in, w_br_moba, w_br_diff, w_out, lambda_q1, lambda_k1, lambda_q2, lambda_k2,
              diff_subln_g, g_mix_pre, g_mix_post, w_up, w_down, g_mlp_pre, g_mlp_post,
              w_ple_proj, w_ple_gate, g_ple_pre, g_ple_post):
    B, S, _ = x.shape
    pos_f = jnp.arange(S, dtype=F32)
    widths = [MOBA_WIDTH, MOBA_WIDTH, MOBA_WIDTH, DIFF_QK_WIDTH, DIFF_QK_WIDTH, DIFF_V_WIDTH, D_MODEL]
    split_points = [int(v) for v in np.cumsum(widths)]
    h = x
    for i in range(DEPTH):
        lambda_init = 0.8 - 0.6 * math.exp(-0.3 * i)
        u = rmsnorm(h, g_mix_pre[i])
        proj = u @ w_in[i]
        qa, ka, va, qb, kb, vb, ga, gb = jnp.split(proj, split_points, axis=-1)
        to_heads = lambda t: t.reshape(B, S, MOBA_HEADS, HEAD_DIM).transpose(0, 2, 1, 3)
        qa = partial_rope(to_heads(qa), pos_f)
        ka = partial_rope(to_heads(ka), pos_f)
        va = to_heads(va)
        oa = moba_attention(qa, ka, va)
        to_sub = lambda t: t.reshape(B, S, DIFF_HEADS, 2, HEAD_DIM).transpose(0, 2, 3, 1, 4)
        qb = partial_rope(to_sub(qb), pos_f)
        kb = partial_rope(to_sub(kb), pos_f)
        vb = vb.reshape(B, S, DIFF_HEADS, DIFF_V_DIM).transpose(0, 2, 1, 3)
        lam = (jnp.exp(jnp.sum(lambda_q1[i].astype(F32) * lambda_k1[i].astype(F32)))
               - jnp.exp(jnp.sum(lambda_q2[i].astype(F32) * lambda_k2[i].astype(F32)))
               + lambda_init)
        ob = diff_attention(qb, kb, vb, lam, diff_subln_g[i], lambda_init)
        ya = oa.transpose(0, 2, 1, 3).reshape(B, S, MOBA_WIDTH) @ w_br_moba[i]
        yb = ob.transpose(0, 2, 1, 3).reshape(B, S, DIFF_V_WIDTH) @ w_br_diff[i]
        mixed = jax.nn.sigmoid(ga) * ya + jax.nn.sigmoid(gb) * yb
        h = h + rmsnorm(mixed @ w_out[i], g_mix_post[i])
        u2 = rmsnorm(h, g_mlp_pre[i])
        ff = jnp.square(jax.nn.relu(u2 @ w_up[i])) @ w_down[i]
        h = h + rmsnorm(ff, g_mlp_post[i])
        gate = jax.nn.sigmoid(rmsnorm(h, g_ple_pre[i]) @ w_ple_gate[i])
        e = (p[i] @ w_ple_proj[i]) * gate
        h = h + rmsnorm(e, g_ple_post[i])
    return h


D_MIX = D_MODEL
MLSTM_HEADS = 4
MLSTM_HEAD_DIM = (D_MIX // 2) // MLSTM_HEADS
MLSTM_WIDTH = MLSTM_HEADS * MLSTM_HEAD_DIM
MLSTM_CHUNK = 64
FOX_HEADS = 8
FOX_HEAD_DIM = (D_MIX - MLSTM_WIDTH) // FOX_HEADS
FOX_WIDTH = FOX_HEADS * FOX_HEAD_DIM
FOX_BLOCK = 128
D_FF_2 = ((8 * D_MODEL // 3 + 255) // 256) * 256
CONV_WIDTH = 3
EPS = 1e-6
IN_SIZES = (MLSTM_WIDTH, MLSTM_WIDTH, MLSTM_WIDTH, MLSTM_WIDTH, MLSTM_HEADS, MLSTM_HEADS,
            FOX_WIDTH, FOX_WIDTH, FOX_WIDTH, FOX_HEADS)
IN_TOTAL = sum(IN_SIZES)


def rms_norm(x, g):
    xf = x.astype(jnp.float32)
    y = xf * lax.rsqrt(jnp.mean(xf * xf, axis=-1, keepdims=True) + EPS)
    return (y * g.astype(jnp.float32)).astype(x.dtype)

def mlstm_chunkwise(q, k, v, ig, lf):
    B, H, S, d = q.shape
    L = MLSTM_CHUNK
    nc = S // L
    k = k * (d ** -0.5)

    def to_chunks(t):
        return jnp.moveaxis(t.reshape((B, H, nc, L) + t.shape[3:]), 2, 0)

    qc, kc, vc = to_chunks(q), to_chunks(k), to_chunks(v)
    igc = to_chunks(ig)
    bc = jnp.cumsum(to_chunks(lf), axis=-1)
    causal = jnp.tril(jnp.ones((L, L), dtype=bool))

    def step(carry, inp):
        C, n, m = carry
        qi, ki, vi, ii, bi = inp
        inter = bi + m[..., None]
        D = jnp.where(causal, bi[..., :, None] - bi[..., None, :] + ii[..., None, :], -jnp.inf)
        m_comb = jnp.maximum(inter, jnp.max(D, axis=-1))
        w_intra = jnp.exp(D - m_comb[..., None])
        w_inter = jnp.exp(inter - m_comb)
        s = jnp.einsum('bhtd,bhsd->bhts', qi, ki) * w_intra
        num = jnp.einsum('bhts,bhsv->bhtv', s, vi) + w_inter[..., None] * jnp.einsum('bhtk,bhkv->bhtv', qi, C)
        den = jnp.sum(s, axis=-1) + w_inter * jnp.einsum('bhtk,bhk->bht', qi, n)
        h = num / jnp.maximum(jnp.abs(den), jnp.exp(-m_comb))[..., None]
        bL = bi[..., -1]
        g = bL[..., None] - bi + ii
        m_new = jnp.maximum(bL + m, jnp.max(g, axis=-1))
        wk = jnp.exp(g - m_new[..., None])
        decay = jnp.exp(bL + m - m_new)
        C = decay[..., None, None] * C + jnp.einsum('bhsk,bhsv->bhkv', ki * wk[..., None], vi)
        n = decay[..., None] * n + jnp.einsum('bhs,bhsk->bhk', wk, ki)
        return (C, n, m_new), h

    init = (jnp.zeros((B, H, d, d), jnp.float32), jnp.zeros((B, H, d), jnp.float32),
            jnp.zeros((B, H), jnp.float32))
    _, hs = lax.scan(step, init, (qc, kc, vc, igc, bc))
    return jnp.moveaxis(hs, 0, 2).reshape(B, H, S, d)

def forgetting_attention(q, k, v, logf):
    B, S, H, d = q.shape
    nb = S // FOX_BLOCK
    F = jnp.cumsum(logf, axis=1).transpose(0, 2, 1)
    kt = k.transpose(0, 2, 1, 3)
    vt = v.transpose(0, 2, 1, 3)
    qb = q.reshape(B, nb, FOX_BLOCK, H, d).transpose(1, 0, 3, 2, 4)
    Fq = F.reshape(B, H, nb, FOX_BLOCK).transpose(2, 0, 1, 3)
    kpos = jnp.arange(S)
    scale = d ** -0.5

    def one_block(args):
        qi, Fqi, bi = args
        qpos = bi * FOX_BLOCK + jnp.arange(FOX_BLOCK)
        s = jnp.einsum('bhqd,bhkd->bhqk', qi, kt, preferred_element_type=jnp.float32) * scale
        s = s + Fqi[..., None] - F[:, :, None, :]
        s = jnp.where(kpos[None, :] <= qpos[:, None], s, -jnp.inf)
        pr = jax.nn.softmax(s, axis=-1)
        return jnp.einsum('bhqk,bhkd->bhqd', pr.astype(vt.dtype), vt)

    out = lax.map(one_block, (qb, Fq, jnp.arange(nb)))
    return out.transpose(1, 0, 3, 2, 4).reshape(B, S, H * d)

def causal_dwconv(a, w, b):
    y = lax.conv_general_dilated(a, w[:, None, :].astype(a.dtype), window_strides=(1,),
                                 padding=[(CONV_WIDTH - 1, 0)],
                                 dimension_numbers=('NWC', 'WIO', 'NWC'),
                                 feature_group_count=a.shape[-1])
    return y + b.astype(a.dtype)

def second_inputs(seed: int = 0) -> dict:
    key = jax.random.key(seed)
    ks = jax.random.split(key, 20)
    nrm = jax.random.normal
    f32 = jnp.float32
    x = nrm(ks[0], (BATCH, SEQ, D_MODEL), f32)
    p = nrm(ks[1], (DEPTH, BATCH, SEQ, PLE_DIM), f32)
    mix_norm_g = 1.0 + 0.02 * nrm(ks[2], (DEPTH, D_MODEL), f32)
    w_in = nrm(ks[3], (DEPTH, D_MODEL, IN_TOTAL), f32) * D_MODEL ** -0.5
    m_i_bias = 0.1 * nrm(ks[4], (DEPTH, MLSTM_HEADS), f32)
    m_f_bias = jnp.linspace(3.0, 6.0, MLSTM_HEADS, dtype=f32)[None, :] + 0.01 * nrm(ks[5], (DEPTH, MLSTM_HEADS), f32)
    mlstm_gate_bias = jnp.concatenate([m_i_bias, m_f_bias], axis=-1)
    mlstm_out_g = 1.0 + 0.02 * nrm(ks[6], (DEPTH, MLSTM_WIDTH), f32)
    fox_q_g = 1.0 + 0.02 * nrm(ks[7], (DEPTH, FOX_HEAD_DIM), f32)
    fox_k_g = 1.0 + 0.02 * nrm(ks[8], (DEPTH, FOX_HEAD_DIM), f32)
    fox_f_bias = jnp.linspace(1.0, 5.0, FOX_HEADS, dtype=f32)[None, :] + 0.01 * nrm(ks[9], (DEPTH, FOX_HEADS), f32)
    w_out = nrm(ks[10], (DEPTH, D_MIX, D_MODEL), f32) * D_MIX ** -0.5
    ffn_norm_g = 1.0 + 0.02 * nrm(ks[11], (DEPTH, D_MODEL), f32)
    w_up = nrm(ks[12], (DEPTH, D_MODEL, 2 * D_FF_2), f32) * D_MODEL ** -0.5
    conv_w = nrm(ks[13], (DEPTH, CONV_WIDTH, D_FF_2), f32) * CONV_WIDTH ** -0.5
    conv_b = 0.02 * nrm(ks[14], (DEPTH, D_FF_2), f32)
    w_down = nrm(ks[15], (DEPTH, D_FF_2, D_MODEL), f32) * D_FF_2 ** -0.5
    ple_norm_g = 1.0 + 0.02 * nrm(ks[16], (DEPTH, D_MODEL), f32)
    w_ple_gate = nrm(ks[17], (DEPTH, D_MODEL, D_MODEL), f32) * D_MODEL ** -0.5
    w_ple_proj = nrm(ks[18], (DEPTH, PLE_DIM, D_MODEL), f32) * PLE_DIM ** -0.5
    return {"x": x, "p": p, "mix_norm_g": mix_norm_g, "w_in": w_in,
            "mlstm_gate_bias": mlstm_gate_bias, "mlstm_out_g": mlstm_out_g,
            "fox_q_g": fox_q_g, "fox_k_g": fox_k_g, "fox_f_bias": fox_f_bias,
            "w_out": w_out, "ffn_norm_g": ffn_norm_g, "w_up": w_up, "conv_w": conv_w,
            "conv_b": conv_b, "w_down": w_down, "ple_norm_g": ple_norm_g,
            "w_ple_gate": w_ple_gate, "w_ple_proj": w_ple_proj}

def second_block(x, p, mix_norm_g, w_in, mlstm_gate_bias, mlstm_out_g, fox_q_g, fox_k_g, fox_f_bias,
              w_out, ffn_norm_g, w_up, conv_w, conv_b, w_down, ple_norm_g, w_ple_gate, w_ple_proj):
    B, S, _ = x.shape
    f32 = jnp.float32
    split_points = np.cumsum(IN_SIZES)[:-1].tolist()
    for i in range(DEPTH):
        h = rms_norm(x, mix_norm_g[i])
        z = h @ w_in[i]
        mq, mk, mv, mo, mi, mf, fq, fk, fv, ff = jnp.split(z, split_points, axis=-1)

        def heads_a(t):
            return t.reshape(B, S, MLSTM_HEADS, MLSTM_HEAD_DIM).transpose(0, 2, 1, 3).astype(f32)
        ig = (mi + mlstm_gate_bias[i, :MLSTM_HEADS]).astype(f32).transpose(0, 2, 1)
        lf = jax.nn.log_sigmoid((mf + mlstm_gate_bias[i, MLSTM_HEADS:]).astype(f32)).transpose(0, 2, 1)
        ha = mlstm_chunkwise(heads_a(mq), heads_a(mk), heads_a(mv), ig, lf)
        ha = rms_norm(ha.transpose(0, 2, 1, 3), mlstm_out_g[i].reshape(MLSTM_HEADS, MLSTM_HEAD_DIM))
        ha = (ha.reshape(B, S, MLSTM_WIDTH) * jax.nn.sigmoid(mo.astype(f32))).astype(x.dtype)

        qb = rms_norm(fq.reshape(B, S, FOX_HEADS, FOX_HEAD_DIM), fox_q_g[i])
        kb = rms_norm(fk.reshape(B, S, FOX_HEADS, FOX_HEAD_DIM), fox_k_g[i])
        vb = fv.reshape(B, S, FOX_HEADS, FOX_HEAD_DIM)
        logf = jax.nn.log_sigmoid((ff + fox_f_bias[i]).astype(f32))
        hb = forgetting_attention(qb, kb, vb, logf).astype(x.dtype)

        x = x + jnp.concatenate([ha, hb], axis=-1) @ w_out[i]

        h = rms_norm(x, ffn_norm_g[i])
        u = h @ w_up[i]
        a, g = jnp.split(u, 2, axis=-1)
        a = causal_dwconv(a, conv_w[i], conv_b[i])
        x = x + (jax.nn.gelu(a, approximate=False) * g) @ w_down[i]

        gate = jax.nn.sigmoid(rms_norm(x, ple_norm_g[i]) @ w_ple_gate[i])
        x = x + gate * (p[i].astype(x.dtype) @ w_ple_proj[i])
    return x


def setup_inputs(seed=0):
    out = dict(first_inputs(seed))
    for name, value in second_inputs(seed + 1).items():
        if name != "x":
            out[name + "_2"] = value
    return out


def reference(
    x, p, w_in, w_br_moba, w_br_diff, w_out, lambda_q1, lambda_k1, lambda_q2, lambda_k2,
    diff_subln_g, g_mix_pre, g_mix_post, w_up, w_down, g_mlp_pre, g_mlp_post, w_ple_proj,
    w_ple_gate, g_ple_pre, g_ple_post, p_2, mix_norm_g_2, w_in_2, mlstm_gate_bias_2,
    mlstm_out_g_2, fox_q_g_2, fox_k_g_2, fox_f_bias_2, w_out_2, ffn_norm_g_2, w_up_2, conv_w_2,
    conv_b_2, w_down_2, ple_norm_g_2, w_ple_gate_2, w_ple_proj_2,
):
    x = first_block(
        x, p, w_in, w_br_moba, w_br_diff, w_out, lambda_q1, lambda_k1, lambda_q2, lambda_k2,
        diff_subln_g, g_mix_pre, g_mix_post, w_up, w_down, g_mlp_pre, g_mlp_post, w_ple_proj,
        w_ple_gate, g_ple_pre, g_ple_post,
    )
    return second_block(
        x, p_2, mix_norm_g_2, w_in_2, mlstm_gate_bias_2, mlstm_out_g_2, fox_q_g_2, fox_k_g_2,
        fox_f_bias_2, w_out_2, ffn_norm_g_2, w_up_2, conv_w_2, conv_b_2, w_down_2, ple_norm_g_2,
        w_ple_gate_2, w_ple_proj_2,
    )


_drawn_inputs = setup_inputs


def setup_inputs(seed=0):
    import zlib

    import numpy as np

    out = dict(_drawn_inputs(seed))
    spreads = {}
    factors = {'diff_subln_g': 3.875,
     'g_mix_post': 4.005,
     'g_mlp_pre': 4.309,
     'g_mlp_post': 5.126,
     'g_ple_pre': 8.0,
     'g_ple_post': 5.414,
     'mix_norm_g_2': 6.448,
     'mlstm_out_g_2': 47.173,
     'fox_q_g_2': 8.0,
     'fox_k_g_2': 8.0,
     'ffn_norm_g_2': 6.694,
     'conv_b_2': 8.0,
     'ple_norm_g_2': 64.0,
     'p_2': 2.802,
     'w_ple_gate_2': 4.215,
     'w_ple_proj_2': 2.804}
    for name, (base, spread) in spreads.items():
        noise = np.random.default_rng([zlib.crc32(name.encode()), seed]).standard_normal(out[name].shape)
        drawn = base * np.exp(spread * noise) if base else spread * noise
        out[name] = __import__('jax').numpy.asarray(drawn.astype(out[name].dtype))
    for name, factor in factors.items():
        out[name] = (out[name] * factor).astype(out[name].dtype)
    return out
```

```python
from contextlib import ExitStack

import numpy as np

import concourse.bass as bass
from concourse import mybir

F32 = mybir.dt.float32
F32R = mybir.dt.float32r
ALU = mybir.AluOpType
ACT = mybir.ActivationFunctionType
AX = mybir.AxisListType

P = 128
TOK = 256
DM = 2048
KT = DM // P
COL = 256
RING = 4
HALF = 4
LEAD = 3
HEADS1 = 8
FF1 = 8192
FF2 = 5632
FFT2 = FF2 // P
EPS = 1e-6
LAMBDA_INIT = 0.2
SCALE = 128 ** -0.5
MLSTM_SCALE = 256 ** -0.5
MASKED = -1e30

CONST_COLS = {}


def constants():
    parts, at = [], 0

    def put(name, a):
        nonlocal at
        full = np.zeros((P, a.shape[1]), np.float32)
        full[: a.shape[0]] = a
        CONST_COLS[name] = (at, at + a.shape[1])
        at += a.shape[1]
        parts.append(full)

    r = np.arange(P)
    put("ident", np.eye(P, dtype=np.float32))
    diag = np.where(r[None, :] <= r[:, None], 0.0, MASKED).astype(np.float32)
    put("mask", np.concatenate([diag, np.zeros((P, P), np.float32), diag], 1))
    put("mask_t", np.concatenate([diag.T, np.zeros((P, P), np.float32), diag.T], 1))
    upper = (r[:, None] <= r[None, :]).astype(np.float32)
    put("tri_ones", np.concatenate([upper, np.ones((P, P), np.float32)], 1))
    rot_dim = 32
    half = rot_dim // 2
    inv = (np.float32(1.0) / (np.float32(500000.0) ** (np.arange(half, dtype=np.float32) * np.float32(2.0) / np.float32(rot_dim)))).astype(np.float32)
    ang = (np.arange(TOK, dtype=np.float32)[None, :] * inv[:, None]).astype(np.float32).astype(np.float64)
    put("cos", np.tile(np.cos(ang), (2, 1)).astype(np.float32))
    put("sin", np.tile(np.sin(ang), (2, 1)).astype(np.float32))
    rot = np.zeros((rot_dim, P), np.float32)
    for m in range(half):
        rot[m + half, m] = -1.0
        rot[m, m + half] = 1.0
    put("rot", rot)
    return np.concatenate(parts, 1)


CONSTANTS = constants()
NCONST = CONSTANTS.shape[1]

PHASES = [
    ("moba", 4, 8, 4), ("diff", 4, 8, 4), ("branch", 4, 8, 6), ("out1", 4, 4, 2),
    ("ffn1", 4, 32, 16), ("proj1", 1, 2, 8), ("gate1", 4, 4, 2),
    ("mlstm", 4, 8, 4), ("fox", 2, 12, 6), ("out2", 4, 4, 2),
    ("ffn2", 2, 48, 24), ("ffn2b", 1, 40, 20), ("proj2", 1, 2, 8), ("gate2", 4, 4, 2),
]
G0, U0 = {}, {}
_g = _u = 0
for _name, _n, _pg, _pu in PHASES:
    G0[_name], U0[_name] = _g, _u
    _g += _n * _pg
    _u += _n * _pu
GRANULES = _g


class At:

    def __init__(self, name, i=0, per_g=0, per_u=0, g=0, u=0, outer_turn=0, outer_units=0):
        self.g, self.u = G0[name] + g, U0[name] + u
        self.turn = i * (per_g // RING) + outer_turn
        self.units = i * per_u + outer_units

    def halves(self, m):
        return 2 * self.g + m + 2 * RING * self.turn

    def unit(self, u):
        return self.u + u + self.units


class Chain:

    def __init__(self, sem):
        self.sem, self.n, self.dyn = sem, 0, 0

    def step(self, ins):
        ins.then_inc(self.sem, 1)
        self.n += 1

    def done(self):
        return self.n + self.dyn


def loop(eng, chain, count, steps, body, start=0):
    first, outer = chain.n, chain.dyn
    with eng.Fori(start, count) as i:
        chain.dyn = outer + (i - start) * steps if steps else outer
        body(i)
    assert chain.n - first == steps, (eng, chain.n - first, steps)
    chain.n = first + (count - start) * steps
    chain.dyn = outer


INPUTS = [
    "x", "p", "w_in", "w_br_moba", "w_br_diff", "w_out", "lambda_q1", "lambda_k1", "lambda_q2", "lambda_k2",
    "diff_subln_g", "g_mix_pre", "g_mix_post", "w_up", "w_down", "g_mlp_pre", "g_mlp_post", "w_ple_proj",
    "w_ple_gate", "g_ple_pre", "g_ple_post", "p_2", "mix_norm_g_2", "w_in_2", "mlstm_gate_bias_2",
    "mlstm_out_g_2", "fox_q_g_2", "fox_k_g_2", "fox_f_bias_2", "w_out_2", "ffn_norm_g_2", "w_up_2", "conv_w_2",
    "conv_b_2", "w_down_2", "ple_norm_g_2", "w_ple_gate_2", "w_ple_proj_2",
]


def over(ap, n):
    return ap.unsqueeze(1).to_broadcast([ap.shape[0], n, ap.shape[1]])


def two_blocks(nc, a, out):
    ctx = ExitStack()

    def sb(name, shape, dt=F32):
        return ctx.enter_context(nc.sbuf_tensor(name, shape, dt))

    def sem(name):
        return ctx.enter_context(nc.semaphore(name))

    raw = sb("raw", [P, RING, 2 * HALF, COL])
    split = sb("split", [P, RING, HALF, 2, COL], F32R)
    h = sb("h", [P, KT, TOK])
    X1 = sb("X1", [P, KT, 2, TOK], F32R)
    X2 = sb("X2", [P, KT, 2, TOK], F32R)
    G = sb("G", [P, KT, TOK])
    E = sb("E", [P, KT, TOK])
    cross = sb("cross", [P, 2, 2, TOK])
    t = sb("t", [P, 2, 2, TOK])
    sg = sb("sg", [P, 2, TOK])[:, :, :]
    con = sb("con", [P, NCONST])
    cols = sb("cols", [P, P + 32 + 4 * FFT2])
    small = sb("small", [P, 64])
    emb = E[:, 14:16, :]
    a_pad = E[:, 0:3, :].rearrange("p a b -> p (a b)")[:, 0:2 * (TOK + 2)].rearrange("p (j t) -> p j t", j=2)
    DK = G[:, 0:3, :].rearrange("p a b -> p (a b)").rearrange("p (h s) -> p h s", h=2)
    acc = sb("acc", [P, 2, TOK])
    rn = sb("rn", [P, 2, TOK])
    sq = rn
    gate_w = sg[:, 0, :].rearrange("p (k c) -> p k c", k=KT)
    gate_split = sb("gate_split", [P, KT, 2, 16], F32R)
    QK = E[:, 0:4, :]
    V = E[:, 4:6, :]
    PR = E[:, 6:9, :].rearrange("p a b -> p (a b)").rearrange("p (h s) -> p h s", h=2)
    PT = E[:, 9:12, :].rearrange("p a b -> p (a b)").rearrange("p (h s) -> p h s", h=2)
    MX = E[:, 12:16, :]
    vec_rows = E[:, 12:14, :].rearrange("p a (b c) -> p (a b) c", b=2)
    x_rows = G[:, :, :].rearrange("p k t -> p (k t)").rearrange("p (a d) -> p a d", a=2)
    out_rows = x_rows
    G_MAX, G_FLOOR, G_DECAY = G[:, 0:4, :], G[:, 4:8, :], G[:, 8:16, :]

    def const(name, rows=P):
        lo, hi = CONST_COLS[name]
        return con[0:rows, lo:hi]

    ident, mask, mask_t, tri = (const(n) for n in ("ident", "mask", "mask_t", "tri_ones"))
    ones = tri[:, P:TOK]
    rope_cos, rope_sin, rot = (const(n, 32) for n in ("cos", "sin", "rot"))

    ps = ctx.enter_context(nc.psum_tensor("ps", [P, 4, 512], F32))
    pw = ctx.enter_context(nc.psum_tensor("pw", [P, 4, 512], F32))

    vectors1 = ["g_mix_pre", "g_mix_post", "g_mlp_pre", "g_mlp_post", "g_ple_pre", "g_ple_post",
                "mix_norm_g_2", "ffn_norm_g_2"]
    col = {n: 16 * k for k, n in enumerate(vectors1)}
    vectors2 = ["ple_norm_g_2", "mlstm_out_g_2", "diff_subln_g", "fox_q_g_2", "fox_k_g_2",
                "lambda_q1", "lambda_k1", "lambda_q2", "lambda_k2"]
    n_rows2 = 0
    for n in vectors2:
        col[n] = P + n_rows2
        n_rows2 += a[n].shape[-1] // P
    assert n_rows2 == 32
    CONV = P + 32
    CONV_BIAS = CONV + 3 * FFT2
    eps_col, neg_lambda, gq_scaled, g_sub_scaled = small[:, 60:61], small[:, 24:25], small[:, 57:58], small[:, 58:60]
    GR = E[:, 8:16, :]
    SEL = G[:, 8:16, :].rearrange("p a b -> p (a b)").rearrange("p (r c) -> p r c", r=16)
    TILES_FFN1, TILES_OUT2, TILES_FFN2 = 1, 33, 41
    GATE_STEPS = 30

    def vec(name, k):
        c = col[name]
        return cols[:, bass.ds(c + k, 1)]

    raw_landed = [sem(f"raw_landed{k}") for k in range(RING)]
    const_landed, x_landed, vec_landed, p_landed = (sem(n) for n in ("const_landed", "x_landed", "vec_landed", "p_landed"))
    gate_w_landed = sem("gate_w_landed")
    pair_used = sem("pair_used")
    hi_done, lo_done, half_used = sem("hi_done"), sem("lo_done"), sem("half_used")
    cross_done, evac_done = sem("cross_done"), sem("evac_done")
    vec_turned, vec_copied = sem("vec_turned"), sem("vec_copied")
    x_turned, eps_ready = sem("x_turned"), sem("eps_ready")
    p_turned, p_hi, p_ready = sem("p_turned"), sem("p_hi"), sem("p_ready")
    lam_parts, lam_summed, lam_exps, lam_ready = (sem(n) for n in ("lam_parts", "lam_summed", "lam_exps", "lam_ready"))
    sums_done, root_done, rn_ready = sem("sums_done"), sem("root_done"), sem("rn_ready")
    h_ready, squares_ready = sem("h_ready"), sem("squares_ready")
    normed, x1_hi, x1_ready = sem("normed"), sem("x1_hi"), sem("x1_ready")
    rot_done, rope_cos_done, rope_done = sem("rot_done"), sem("rope_cos_done"), sem("rope_done")
    scores_done, logits_done, exp_done, probs_ready = (sem(n) for n in ("scores_done", "logits_done", "exp_done", "probs_ready"))
    probs_turned, pt_ready, pv_done = sem("probs_turned"), sem("pt_ready"), sem("pv_done")
    o_raw, o_squares, o_sums, o_root, o_normed, o_hi, o_ready = (sem(n) for n in ("o_raw", "o_squares", "o_sums", "o_root", "o_normed", "o_hi", "o_ready"))
    sig_done, gated, unit_squares, tiles_done = (sem(n) for n in ("sig_done", "gated", "unit_squares", "tiles_done"))
    conv_done, hid_done, hid_hi, hid_ready = (sem(n) for n in ("conv_done", "hid_done", "hid_hi", "hid_ready"))
    gates, gate_split_hi, gate_split_lo = sem("gates"), sem("gate_split_hi"), sem("gate_split_lo")
    wt_arg, wt_done, pt_gated, den_done, den_abs, bias_done = (sem(n) for n in ("wt_arg", "wt_done", "pt_gated", "den_done", "den_abs", "bias_done"))
    qk_squares, qk_sums, qk_root, qk_ready = (sem(n) for n in ("qk_squares", "qk_sums", "qk_root", "qk_ready"))
    out_turned, out_copied, out_landed = sem("out_turned"), sem("out_copied"), sem("out_landed")
    act_steps, dve_steps, pool_steps = sem("act_steps"), sem("dve_steps"), sem("pool_steps")

    def plan(units):
        rows = []
        for u, (form, op, k0, counts) in enumerate(units):
            for q, n in enumerate(counts):
                rows.append((u, form, op, k0 + sum(counts[:q]), n, q == 0, q == len(counts) - 1))
        return rows

    full1 = ("features", X1, 0, (4, 4, 4, 4))
    tokens1 = ("tokens", X1, 0, (4, 4, 4, 4))
    full2 = ("features", X2, 0, (4, 4, 4, 4))
    MIX = plan([full1, full1, tokens1, full1])
    BRANCH = plan(2 * [full1, ("features", X2, 0, (4, 4)), ("features", X2, 8, (4, 4))])
    TWO = plan([full1, full1])
    OUT2 = DOWN = plan([full2, full2])
    DOWN3 = plan(2 * [("features", X2, 0, (4, 2, 4, 2))])
    FOX = plan(2 * [full1, full1, tokens1])

    block = ctx.enter_context(nc.Block())

    @block.sync
    def _(sp):
        def load(at, g, source):
            k = at.g + g
            if not (isinstance(at.turn, int) and k + RING * at.turn < RING):
                sp.wait_ge(lo_done, at.halves(2 * g) - 2 * RING + 2)
            tiles = source.shape[0] // P
            dst = raw[:, k % RING, :, :].rearrange("p k c -> p (k c)")[:, 0:tiles * source.shape[1]]
            sp.dma_start(dst.rearrange("p (k c) -> p k c", k=tiles),
                         source.rearrange("(k p) c -> p k c", p=P)).then_inc(raw_landed[k % RING], 16)

        def unit(at, g, w, col0, row0=0, rows=2048):
            step = rows // 2 if rows >= 1536 else rows
            for q in range(rows // step):
                load(at, g + q, w[bass.ds(row0 + q * step, step), bass.ds(col0, COL)])

        w_in, w_in2 = a["w_in"][0], a["w_in_2"][0]

        def moba(i):
            s = At("moba", i, 8, 4)
            for u, c in enumerate((0, 1024, 2048, 6144)):
                unit(s, 2 * u, w_in, c + i * COL)

        sp.dma_start(con[:, :], a["constants"]).then_inc(const_landed, 16)
        sp.dma_start(x_rows, a["x"][0].rearrange("(a p) d -> p a d", p=P)).then_inc(x_landed, 16)
        moba(0)
        loop(sp, Chain(None), 4, 0, moba, start=1)

        def diff(i):
            s = At("diff", i, 8, 4)
            for u, c in enumerate((3072, 4096, 5120, 6144 + 1024)):
                unit(s, 2 * u, w_in, c + i * COL)
        loop(sp, Chain(None), 4, 0, diff)

        def branch(j):
            s = At("branch", j - 1, 8, 6)
            for n in range(2):
                c = j * (2 * COL) + (n - 2) * COL
                unit(s, 4 * n, w_in, c + 8192)
                unit(s, 4 * n + 2, a["w_br_moba"][0], c, rows=1024)
                unit(s, 4 * n + 3, a["w_br_diff"][0], c, rows=1024)
        loop(sp, Chain(None), 5, 0, branch, start=1)

        def square(name, w):
            def body(i):
                s = At(name, i, 4, 2)
                for u in range(2):
                    unit(s, 2 * u, w, i * (2 * COL) + u * COL)
            loop(sp, Chain(None), 4, 0, body)

        square("out1", a["w_out"][0])

        def ffn1(b):
            def up(i):
                s = At("ffn1", i, 4, 2, outer_turn=b * 8, outer_units=b * 16)
                for u in range(2):
                    unit(s, 2 * u, a["w_up"][0], b * 2048 + i * 512 + u * COL)

            def down(i):
                s = At("ffn1", i, 4, 2, g=16, u=8, outer_turn=b * 8, outer_units=b * 16)
                for u in range(2):
                    unit(s, 2 * u, a["w_down"][0], i * 512 + u * COL, row0=b * 2048)
            loop(sp, Chain(None), 4, 0, up)
            loop(sp, Chain(None), 4, 0, down)
        loop(sp, Chain(None), 4, 0, ffn1)

        def proj(name, w):
            for g in range(2):
                load(At(name), g, w[:, g * 1024:g * 1024 + 1024])
        proj("proj1", a["w_ple_proj"][0])
        square("gate1", a["w_ple_gate"][0])


        w_in_q2 = w_in2

        def mlstm(i):
            s = At("mlstm", i, 8, 4)
            for u, c in enumerate((0, 1024, 2048, 3072)):
                unit(s, 2 * u, w_in_q2, c + i * COL)
        loop(sp, Chain(None), 4, 0, mlstm)

        def fox(i):
            s = At("fox", i, 12, 6)
            for q in range(2):
                for u, c in enumerate((4104, 5128, 6152)):
                    unit(s, 6 * q + 2 * u, w_in_q2, c + q * COL + i * (2 * COL))
        loop(sp, Chain(None), 2, 0, fox)
        square("out2", a["w_out_2"][0])

        def ffn2(name, b, pairs, rows):
            turn, units = (b * 12, b * 24) if name == "ffn2" else (0, 0)
            col0 = b * 2048 if name == "ffn2" else 4096

            def up(i):
                s = At(name, i, 4, 2, outer_turn=turn, outer_units=units)
                unit(s, 0, a["w_up_2"][0], col0 + i * COL)
                unit(s, 2, a["w_up_2"][0], FF2 + col0 + i * COL)

            def down(i):
                s = At(name, i, 4, 2, g=4 * pairs, u=2 * pairs, outer_turn=turn, outer_units=units)
                for u in range(2):
                    unit(s, 2 * u, a["w_down_2"][0], i * 512 + u * COL, row0=col0, rows=rows)
            loop(sp, Chain(None), pairs, 0, up)
            loop(sp, Chain(None), 4, 0, down)
        loop(sp, Chain(None), 2, 0, lambda b: ffn2("ffn2", b, 8, 2048))
        ffn2("ffn2b", 0, 6, 1536)
        proj("proj2", a["w_ple_proj_2"][0])
        square("gate2", a["w_ple_gate_2"][0])
        for k in range(4):
            sp.wait_ge(out_copied, 2 * k + 2)
            sp.dma_start(out[0, (k // 2) * P:(k // 2) * P + P, (k % 2) * 1024:(k % 2) * 1024 + 1024],
                         out_rows[:, k // 2, (k % 2) * 1024:(k % 2) * 1024 + 1024]).then_inc(out_landed, 16)
        sp.wait_ge(out_landed, 64)

    @block.gpsimd
    def _(pool):
        for k, n in enumerate(vectors1):
            pool.dma_start(vec_rows[16 * k:16 * k + 16, 0, :], a[n][0].rearrange("(k c) -> k c", c=P)).then_inc(vec_landed, 16)
        for n in vectors2:
            r0, nr = col[n] - P, a[n].shape[-1] // P
            pool.dma_start(vec_rows[r0:r0 + nr, 1, :], a[n][0].rearrange("(k c) -> k c", c=P)).then_inc(vec_landed, 16)
        for w in range(4):
            src = a["conv_w_2"][0, w] if w < 3 else a["conv_b_2"][0]
            r0 = FFT2 * (w % 2)
            pool.dma_start(vec_rows[r0:r0 + FFT2, 2 + w // 2, :], src.rearrange("(k c) -> k c", c=P)).then_inc(vec_landed, 16)

        steps = Chain(pool_steps)

        def rope(p):
            pool.wait_ge(rot_done, p + 1)
            nc.gpsimd.tensor_tensor(QK[0:32], QK[0:32], over(rope_cos, 4), ALU.mult).then_inc(rope_cos_done, 1)

        rope(0)
        loop(pool, steps, 8, 0, rope, start=1)

        def clear_acc():
            steps.step(nc.gpsimd.memset(acc[:, :, :], 0.0))
            pool.wait_ge(pool_steps, steps.done())

        def sum_units(k0, written, base, tile_of):
            def body(i):
                for u in range(2):
                    pool.wait_ge(written, base + 2 * i + u + 1)
                    src = tile_of(i, u)
                    steps.step(nc.gpsimd.tensor_tensor(sq[:, :, :], src, src, ALU.mult))
                    pool.wait_ge(pool_steps, steps.done())
                    nc.gpsimd.tensor_tensor(acc[:, :, :], acc[:, :, :], sq[:, :, :], ALU.add).then_inc(unit_squares, 1)
                    pool.wait_ge(unit_squares, k0 + 2 * i + u + 1)
            loop(pool, steps, 4, 2, body)

        def g_tile(i, u):
            return G[:, bass.ds(4 * i + 2 * u, 2), :]

        def h_tile(i, u):
            return h[:, bass.ds(4 * i + 2 * u, 2), :]

        clear_acc()
        sum_units(0, evac_done, U0["out1"], g_tile)
        pool.wait_ge(o_ready, 12)
        pool.dma_start(emb[:, :, :], a["p"][0, 0].rearrange("(a p) d -> p a d", p=P)).then_inc(p_landed, 16)
        pool.wait_ge(x1_ready, 12)
        nc.gpsimd.memset(G[:, :, :], 0.0).then_inc(tiles_done, 1)
        clear_acc()
        sum_units(8, tiles_done, TILES_FFN1 + 24, g_tile)
        pool.wait_ge(sums_done, 4)
        clear_acc()
        sum_units(16, gated, 8, g_tile)
        pool.wait_ge(sums_done, 6)
        clear_acc()
        pool.wait_ge(gated, 16)
        w_in2 = a["w_in_2"][0]
        for c0, n, src in ((0, 4, 4100), (4, 8, 7176), (12, 4, 4096)):
            pool.dma_start(gate_w[:, :, c0:c0 + n], w_in2[:, src:src + n].rearrange("(k p) c -> p k c", p=P)).then_inc(gate_w_landed, 16)
        gb = a["mlstm_gate_bias_2"][0]
        for r0, n, src in ((0, 4, gb[4:8]), (4, 8, a["fox_f_bias_2"][0]), (12, 4, gb[0:4])):
            pool.dma_start(small[r0:r0 + n, 40:41], src.rearrange("(k c) -> k c", c=1)).then_inc(gate_w_landed, 16)


        def wt(i):
            pool.wait_ge(gates, GATE_STEPS)
            if not isinstance(i, int):
                pool.wait_ge(pt_gated, i)
            row = G_MAX[:, bass.ds(i, 1), :].rearrange("p a t -> p (a t)")
            steps.step(nc.gpsimd.tensor_tensor(PR[:, 0, 0:TOK], mask_t[:, 0:TOK], row, ALU.subtract))
            row1 = G_MAX[:, bass.ds(i, 1), P:TOK].rearrange("p a t -> p (a t)")
            nc.gpsimd.tensor_tensor(PR[:, 0, TOK:384], mask_t[:, TOK:384], row1, ALU.subtract).then_inc(wt_arg, 1)
        wt(0)
        loop(pool, steps, 4, 1, wt, start=1)

        pool.wait_ge(o_ready, 16)

        def decay(q):
            pool.wait_ge(logits_done, 16 + 2 * q)
            for hh in range(2):
                rows = G_DECAY[:, bass.ds(2 * q + hh, 1), :].rearrange("p a t -> p (a t)")
                first = G_DECAY[:, bass.ds(2 * q + hh, 1), 0:P].rearrange("p a t -> p (a t)")
                steps.step(nc.gpsimd.tensor_tensor(DK[:, hh, 0:P], mask[:, 0:P], first, ALU.add))
                nc.gpsimd.tensor_tensor(DK[:, hh, P:384], mask[:, P:384], rows, ALU.add).then_inc(bias_done, 1)
        loop(pool, steps, 4, 2, decay)

        sum_units(24, tiles_done, TILES_OUT2, h_tile)
        pool.wait_ge(o_ready, 24)
        pool.dma_start(emb[:, :, :], a["p_2"][0, 0].rearrange("(a p) d -> p a d", p=P)).then_inc(p_landed, 16)
        pool.wait_ge(sums_done, 8)
        clear_acc()
        sum_units(32, tiles_done, TILES_FFN2 + 16, h_tile)

    @block.scalar
    def _(act):
        steps = Chain(act_steps)
        A = nc.scalar.activation

        def hi(at, m):
            k = 2 * at.g + m + LEAD
            act.wait_ge(raw_landed[(k // 2) % RING], 16 * (k // 2 // RING + 1) + 16 * at.turn)
            if not (isinstance(at.turn, int) and k + 8 * at.turn < RING):
                act.wait_ge(half_used, k - RING + 1 + 8 * at.turn)
            A(split[:, k % RING, :, 0, :], raw[:, (k // 2) % RING, HALF * (k % 2):HALF * (k % 2) + HALF, :], ACT.Copy).then_inc(hi_done, 1)

        def evac(at, m, u):
            s = (at.u + u) % 2
            act.wait_ge(half_used, at.halves(m) + 1)
            A(cross[:, s], ps[:, 2 * s:2 * s + 2, TOK:512], ACT.Copy).then_inc(cross_done, 1)

        def each_half(at, rows, after, final=False):
            for m, (u, _, _, _, _, _, last) in enumerate(rows):
                if not (final and m + LEAD >= len(rows)):
                    hi(at, m)
                if last:
                    evac(at, m, u)
                after(m)

        def root(k, bank, scale=1.0 / DM):
            act.wait_ge(sums_done, k + 1)
            A(rn[:, 0, :], pw[:, bank, 0:TOK], ACT.Sqrt, bias=eps_col, scale=scale).then_inc(root_done, 1)

        def square_chunks(k, hooks=None):
            for c in range(4):
                act.wait_ge(h_ready, 4 * k + c + 1)
                A(G[:, 4 * c:4 * c + 4, :], h[:, 4 * c:4 * c + 4, :], ACT.Square).then_inc(squares_ready, 1)
                if hooks:
                    hooks[c]()

        def x1_chunks(e, k, hooks=None):
            for c in range(4):
                act.wait_ge(normed, 4 * k + c + 1)
                A(X1[:, 4 * c:4 * c + 4, 0, :], G[:, 4 * c:4 * c + 4, :], ACT.Copy).then_inc(x1_hi, 1)
                if hooks:
                    hooks[c]()

        act.wait_ge(eps_ready, 1)
        for m in range(LEAD):
            hi(At("moba"), m - LEAD)
        for c in range(4):
            act.wait_ge(x_turned, 2 * c + 2)
            A(h[:, 4 * c:4 * c + 4, :].rearrange("p (a b) t -> p a (b t)", a=2), pw[:, 2 * (c % 2):2 * (c % 2) + 2, :], ACT.Copy).then_inc(h_ready, 1)
        act.wait_ge(vec_turned, 1)
        A(cols[:, 0:P + n_rows2], pw[:, 0, 0:P + n_rows2], ACT.Copy).then_inc(vec_copied, 1)
        A(cols[:, P + 32:], pw[:, 1, 0:4 * FFT2], ACT.Copy).then_inc(vec_copied, 1)
        for c in range(4):
            act.wait_ge(h_ready, c + 1)
            A(G[:, 4 * c:4 * c + 4, :], h[:, 4 * c:4 * c + 4, :], ACT.Square).then_inc(squares_ready, 1)
        root(0, 0)
        x1_chunks(0, 0)
        act.wait_ge(lam_summed, 1)
        A(small[:, 22:24], pw[:, 1, 0:2], ACT.Exp).then_inc(lam_exps, 1)

        def softmax_exps(k, heads=2):
            for hh in range(heads):
                act.wait_ge(logits_done, k + hh + 1)
                A(PR[:, hh, 0:P], PR[:, hh, 0:P], ACT.Exp, bias=small[:, 2 * hh:2 * hh + 1], scale=-1.0,
                  accum_out=small[:, 4 + 2 * hh:5 + 2 * hh])
                A(PR[:, hh, P:384], PR[:, hh, P:384], ACT.Exp, bias=small[:, 2 * hh + 1:2 * hh + 2], scale=-1.0,
                  accum_out=small[:, 5 + 2 * hh:6 + 2 * hh]).then_inc(exp_done, 1)

        def copy_pt(k, heads):
            for hh in range(heads):
                act.wait_ge(probs_turned, k + hh + 1)
                A(PT[:, hh, :], pw[:, hh, 0:384], ACT.Copy).then_inc(pt_ready, 1)

        def o_heads(k, tile):
            for hh in range(2):
                act.wait_ge(pv_done, k + hh + 1)
                A(X2[:, bass.ds(tile + hh, 1), 0, :], pw[:, 2 + hh, 0:TOK].unsqueeze(1), ACT.Copy).then_inc(o_hi, 1)

        def o_square(n):
            act.wait_ge(o_raw, n + 1)
            A(MX[:, 2:4, :], MX[:, 0:2, :], ACT.Square).then_inc(o_squares, 1)

        def o_norm(n):
            act.wait_ge(o_sums, n + 1)
            A(rn[:, 0, :], pw[:, 1, 0:TOK], ACT.Sqrt, bias=eps_col, scale=1.0 / 256).then_inc(o_root, 1)

        def o_pair(k, n, tile):
            act.wait_ge(o_normed, n + 1)
            A(X2[:, bass.ds(tile, 2), 0, :], MX[:, 0:2, :], ACT.Copy).then_inc(o_hi, 1)

        def gate_a(at, p):
            act.wait_ge(evac_done, at.unit(3) + 1)
            A(G[:, bass.ds(2 * p, 2), :], t[:, 1], ACT.Sigmoid).then_inc(sig_done, 1)

        def moba(i):
            s = At("moba", i, 8, 4)

            def after(m):
                if m == 11:
                    softmax_exps(2 * i)
                if m == 13:
                    copy_pt(2 * i, 2)
                if m == 15:
                    o_heads(2 * i, 2 * i)
                    gate_a(s, i)
            each_half(s, MIX, after)
        moba(0)
        loop(act, steps, 4, 0, moba, start=1)

        def diff(i):
            s = At("diff", i, 8, 4)

            def after(m):
                if m == 11:
                    softmax_exps(2 * i + 8)
                if m == 13:
                    copy_pt(8 + i, 1)
                if m == 15:
                    o_square(i)
                    gate_a(s, i + 4)
                if m == 2 and not isinstance(i, int):
                    finish_diff(i - 1)
            each_half(s, MIX, after)

        def finish_diff(j):
            o_norm(j)
            o_pair(8 + j, j, 8 + 2 * j)
        diff(0)
        loop(act, steps, 4, 0, diff, start=1)

        def branch(i):
            s = At("branch", i, 8, 6)

            def after(m):
                if m == 2 and isinstance(i, int):
                    finish_diff(3)
                if m in (3, 11):
                    n = m // 8
                    act.wait_ge(evac_done, s.unit(3 * n) + 1)
                    if not (isinstance(i, int) and i + n == 0):
                        act.wait_ge(gated, 2 * i + n)
                    A(sg[:, :, :], t[:, (s.u + 3 * n) % 2], ACT.Sigmoid).then_inc(sig_done, 1)
            each_half(s, BRANCH, after)
        branch(0)
        loop(act, steps, 4, 0, branch, start=1)
        for c in range(4):
            act.wait_ge(gated, 8)
            A(X1[:, 4 * c:4 * c + 4, 0, :], G[:, 4 * c:4 * c + 4, :], ACT.Copy).then_inc(x1_hi, 1)

        def plain(name, rows, g=0, u=0, per=(4, 2), **outer):
            def body(i):
                each_half(At(name, i, *per, g=g, u=u, **outer), rows, lambda m: None)
            return body
        loop(act, steps, 4, 0, plain("out1", TWO))

        root(1, 0)
        square_chunks(1)
        root(2, 0)
        x1_chunks(2, 1)

        def ffn1(b):
            def up(i):
                s = At("ffn1", i, 4, 2, outer_turn=b * 8, outer_units=b * 16)

                def after(m):
                    if m % 4 == 3:
                        u = m // 4
                        k = b * 8 + 2 * i + u
                        act.wait_ge(hid_done, k + 1)
                        A(X2[:, bass.ds(4 * i + 2 * u, 2), 0, :], t[:, (s.u + u) % 2], ACT.Copy).then_inc(hid_hi, 1)
                each_half(s, TWO, after)
            loop(act, steps, 4, 0, up)
            loop(act, steps, 4, 0, plain("ffn1", DOWN, 16, 8, outer_turn=b * 8, outer_units=b * 16))
        loop(act, steps, 4, 0, ffn1)

        def embed(k):
            act.wait_ge(p_turned, k + 1)
            A(X2[:, 0:2, 0, :], pw[:, 2, :].rearrange("p (a t) -> p a t", a=2), ACT.Copy).then_inc(p_hi, 1)

        def proj_granule(at, g, k):
            hi(at, 2 * g)
            for c in range(4):
                if c == 2:
                    hi(at, 2 * g + 1)
                if c < 3:
                    act.wait_ge(pair_used, 3 * k + c + 1)
                    s = (at.u + 4 * g + c) % 2
                    A(cross[:, s], ps[:, 2 * s:2 * s + 2, TOK:512], ACT.Copy).then_inc(cross_done, 1)
                else:
                    evac(at, 2 * g + 1, 4 * g + c)

        s = At("proj1")
        embed(0)
        proj_granule(s, 0, 0)
        root(3, 0)
        square_chunks(2, [lambda: None, lambda: proj_granule(s, 1, 1), lambda: None, lambda: None])
        root(4, 0)
        x1_chunks(3, 2)

        def gate(name, used, final=False):
            def body(i):
                s = At(name, i, 4, 2)

                def after(m):
                    if m % 4 == 3:
                        u = m // 4
                        act.wait_ge(evac_done, s.unit(u) + 1)
                        act.wait_ge(gated, used + 2 * i + u)
                        A(sg[:, :, :], t[:, (s.u + u) % 2], ACT.Sigmoid).then_inc(sig_done, 1)
                each_half(s, TWO, after, final)
            return body
        loop(act, steps, 4, 0, gate("gate1", 8))

        root(5, 0)
        square_chunks(3)
        root(6, 0)
        x1_chunks(4, 3)

        def gate_step(k, out_, in_, func, **more):
            act.wait_ge(gates, k - 1)
            A(out_, in_, func, **more).then_inc(gates, 1)
        act.wait_ge(gate_w_landed, 96)
        A(gate_split[:, :, 0, :], gate_w[:, :, :], ACT.Copy).then_inc(gate_split_hi, 1)
        def gate_steps(m):
            if m == 4:
                gate_step(2, GR[0:16, 0], pw[0:16, 0, TOK:512], ACT.Copy)
                gate_step(5, GR[0:16, 2], GR[0:16, 1], ACT.Abs)
                gate_step(6, GR[0:16, 2], GR[0:16, 2], ACT.Exp, scale=-1.0)
                gate_step(7, GR[0:16, 2], GR[0:16, 2], ACT.Ln, bias=1.0)
            if m == 6:
                gate_step(10, small[:, 0:32], pw[:, 1, 0:32], ACT.Copy)
            if m == 7:
                gate_step(12, GR[0:16, 4], pw[0:16, 2, 0:TOK], ACT.Copy)
            if m == 9:
                gate_step(23, GR[0:4, 3], GR[0:4, 2], ACT.Exp, scale=-1.0)
                gate_step(25, small[:, 48:56], pw[:, 0, 0:8], ACT.Copy)
            if m == 10:
                gate_step(27, G_MAX.rearrange("p (a b) t -> p a (b t)", a=2), pw[:, 0:2, :], ACT.Copy)
                gate_step(28, G_FLOOR.rearrange("p (a b) t -> p a (b t)", a=2), pw[:, 2:4, :], ACT.Copy)
            if m == 11:
                gate_step(30, G_DECAY.rearrange("p (a b) t -> p a (b t)", a=4), pw[:, :, :], ACT.Copy, scale=-1.0)

        def mlstm(i):
            s = At("mlstm", i, 8, 4)

            first = isinstance(i, int)

            def after(m):
                if first:
                    gate_steps(m)
                elif m == 2:
                    finish_mlstm(i - 1)
                if m == (12 if first else 5):
                    act.wait_ge(wt_arg, i + 1)
                    A(PR[:, 0, 0:TOK], PR[:, 0, 0:TOK], ACT.Exp, bias=small[:, bass.ds(48 + i, 1)])
                    A(PR[:, 0, TOK:384], PR[:, 0, TOK:384], ACT.Exp, bias=small[:, bass.ds(52 + i, 1)]).then_inc(wt_done, 1)
                if m == (14 if first else 13):
                    act.wait_ge(den_done, i + 1)
                    A(rn[:, 0, :], pw[:, 1, 0:TOK], ACT.Abs).then_inc(den_abs, 1)
                    o_square(i + 4)
                if m == 15:
                    act.wait_ge(evac_done, s.unit(3) + 1)
                    A(sg[:, :, :], t[:, (s.u + 3) % 2], ACT.Sigmoid).then_inc(sig_done, 1)
            each_half(s, MIX, after)

        def finish_mlstm(j):
            o_norm(j + 4)
            o_pair(12 + j, j + 4, 2 * j)
        mlstm(0)
        loop(act, steps, 4, 0, mlstm, start=1)

        def fox(i):
            s = At("fox", i, 12, 6)

            def square_qk(r):
                act.wait_ge(evac_done, s.unit(3 * r + 1) + 1)
                A(MX, QK, ACT.Square).then_inc(qk_squares, 1)

            def root_qk(q):
                act.wait_ge(qk_sums, q + 1)
                A(MX.rearrange("p (a b) t -> p a (b t)", a=2), pw[:, 0:2, :], ACT.Sqrt, bias=eps_col, scale=1.0 / P).then_inc(qk_root, 1)

            def after(m):
                r, q = m // 12, 2 * i + m // 12
                if m in (7, 19):
                    square_qk(r)
                if m == 9:
                    root_qk(q)
                if m == 12:
                    softmax_exps(16 + 4 * i)
                if m == 14:
                    copy_pt(12 + 4 * i, 2)
                if m == 16:
                    o_heads(16 + 4 * i, 8 + 4 * i)
                if m == 21:
                    root_qk(q)
                if m == 23:
                    softmax_exps(18 + 4 * i)
                if i == 0 and m == 2:
                    finish_mlstm(3)
                if i == 1:
                    finish_fox(0, m)
            each_half(s, FOX, after)

        def finish_fox(j, m):
            if m == 1:
                copy_pt(14 + 4 * j, 2)
            if m == 2:
                o_heads(18 + 4 * j, 10 + 4 * j)
        fox(0)
        fox(1)
        each_half(At("out2"), TWO, lambda m: finish_fox(1, m))
        loop(act, steps, 4, 0, plain("out2", TWO), start=1)

        root(7, 0)
        x1_chunks(5, 4)

        def ffn2(name, b, pairs, k0):
            turn, units = (b * 12, b * 24) if name == "ffn2" else (0, 0)

            def up(i):
                s = At(name, i, 4, 2, outer_turn=turn, outer_units=units)

                def after(m):
                    if m == 5:
                        act.wait_ge(conv_done, k0 + i + 1)
                        for j in range(2):
                            bias = cols[:, bass.ds(CONV_BIAS + (b * 16 if name == "ffn2" else 32) + 2 * i + j, 1)]
                            ins = A(sg[:, j, :], t[:, s.u % 2, j, :], ACT.Gelu, bias=bias)
                        ins.then_inc(sig_done, 1)
                    if m == 7:
                        act.wait_ge(hid_done, 32 + k0 + i + 1)
                        A(X2[:, bass.ds(2 * i, 2), 0, :], t[:, (s.u + 1) % 2], ACT.Copy).then_inc(hid_hi, 1)
                each_half(s, TWO, after)
            loop(act, steps, pairs, 0, up)
            rows = DOWN if name == "ffn2" else DOWN3
            loop(act, steps, 4, 0, plain(name, rows, 4 * pairs, 2 * pairs, outer_turn=turn, outer_units=units))
        loop(act, steps, 2, 0, lambda b: ffn2("ffn2", b, 8, b * 8))
        ffn2("ffn2b", 0, 6, 16)

        s2 = At("proj2")
        embed(1)
        proj_granule(s2, 0, 2)
        root(8, 0)
        x1_chunks(6, 5, [lambda: None, lambda: proj_granule(s2, 1, 3), lambda: None, lambda: None])

        loop(act, steps, 3, 0, gate("gate2", 16))
        gate("gate2", 16, final=True)(3)
        for k in range(8):
            act.wait_ge(out_turned, k + 1)
            A(out_rows[:, k // 4, (k % 4) * 512:(k % 4) * 512 + 512], pw[:, k % 4, :], ACT.Copy).then_inc(out_copied, 1)

    @block.vector
    def _(dve):
        steps = Chain(dve_steps)
        TT, STT = nc.vector.tensor_tensor, nc.vector.scalar_tensor_tensor

        def settled():
            dve.wait_ge(dve_steps, steps.done())

        def lo(at, m):
            k = 2 * at.g + m + LEAD
            dve.wait_ge(hi_done, k + 1 + 8 * at.turn)
            TT(split[:, k % RING, :, 1, :], raw[:, (k // 2) % RING, HALF * (k % 2):HALF * (k % 2) + HALF, :],
               split[:, k % RING, :, 0, :], ALU.subtract).then_inc(lo_done, 1)

        def evac(at, u, dst):
            s = (at.u + u) % 2
            dve.wait_ge(cross_done, at.unit(u) + 1)
            TT(dst, ps[:, 2 * s:2 * s + 2, 0:TOK], cross[:, s], ALU.add).then_inc(evac_done, 1)

        def evaced(at, u):
            dve.wait_ge(evac_done, at.unit(u) + 1)

        def each_half(at, rows, after, final=False):
            for m in range(len(rows)):
                if not (final and m + LEAD >= len(rows)):
                    lo(at, m)
                after(m)

        def inverse_root(k):
            dve.wait_ge(root_done, k + 1)
            nc.vector.reciprocal(rn[:, 1, :], rn[:, 0, :]).then_inc(rn_ready, 1)
            dve.wait_ge(rn_ready, k + 1)

        def post_norm(k, gain, hooks=None):
            for c in range(4):
                for kt in range(4 * c, 4 * c + 4):
                    steps.step(STT(G[:, kt, :], G[:, kt, :], vec(gain, kt), rn[:, 1, :], ALU.mult, ALU.mult))
                settled()
                TT(h[:, 4 * c:4 * c + 4, :], h[:, 4 * c:4 * c + 4, :], G[:, 4 * c:4 * c + 4, :], ALU.add).then_inc(h_ready, 1)
                if hooks:
                    hooks[c]()

        def x1_lo(e, c):
            dve.wait_ge(x1_hi, 4 * e + c + 1)
            TT(X1[:, 4 * c:4 * c + 4, 1, :], G[:, 4 * c:4 * c + 4, :], X1[:, 4 * c:4 * c + 4, 0, :], ALU.subtract).then_inc(x1_ready, 1)

        def pre_norm(e, gain, hooks=None):
            for c in range(4):
                for kt in range(4 * c, 4 * c + 4):
                    ins = STT(G[:, kt, :], h[:, kt, :], vec(gain, kt), rn[:, 1, :], ALU.mult, ALU.mult)
                ins.then_inc(normed, 1)
                if c:
                    x1_lo(e, c - 1)
                if hooks:
                    hooks[c]()
            x1_lo(e, 3)

        nc.vector.memset(eps_col, EPS).then_inc(eps_ready, 1)
        for m in range(LEAD):
            lo(At("moba"), m - LEAD)
        dve.wait_ge(vec_copied, 2)
        c = col["lambda_q1"]
        steps.step(TT(small[:, 20:21], cols[:, c:c + 1], cols[:, c + 1:c + 2], ALU.mult))
        TT(small[:, 21:22], cols[:, c + 2:c + 3], cols[:, c + 3:c + 4], ALU.mult).then_inc(lam_parts, 1)
        c = col["diff_subln_g"]
        steps.step(nc.vector.tensor_scalar(g_sub_scaled, cols[:, c:c + 2], 1.0 - LAMBDA_INIT, None, ALU.mult))
        c = col["fox_q_g_2"]
        steps.step(nc.vector.tensor_scalar(gq_scaled, cols[:, c:c + 1], SCALE, None, ALU.mult))
        inverse_root(0)
        pre_norm(0, "g_mix_pre")
        dve.wait_ge(lam_exps, 1)
        steps.step(STT(neg_lambda, small[:, 23:24], -LAMBDA_INIT, small[:, 22:23], ALU.add, ALU.subtract))
        settled()

        def rope(p):
            dve.wait_ge(rot_done, p + 1)
            steps.step(TT(MX[0:32], pw[0:32, 0:2, :].rearrange("p a (b t) -> p (a b) t", b=2), over(rope_sin, 4), ALU.mult))
            settled()
            dve.wait_ge(rope_cos_done, p + 1)
            TT(QK[0:32], QK[0:32], MX[0:32], ALU.add).then_inc(rope_done, 1)

        def logits(scores, k, tables, scale):
            for hh in range(2):
                dve.wait_ge(scores_done, scores + hh + 1)
                table = tables(hh)
                steps.step(nc.vector.memset(small[:, 16 + hh:17 + hh], 0.0))
                for q, (a0, a1) in enumerate(((0, P), (P, 384))):
                    ins = nc.vector.tensor_tensor_reduce(
                        out=PR[:, hh, a0:a1], in0=pw[:, 2 + hh, a0:a1], in1=table[:, a0:a1], scale=-scale, scalar=3e38,
                        op0=ALU.add, op1=ALU.min, accum_out=small[:, 2 * hh + q:2 * hh + q + 1])
                ins.then_inc(logits_done, 1)

        def normalise(k, kp):
            for hh in range(2):
                dve.wait_ge(exp_done, k + hh + 1)
                steps.step(nc.vector.reciprocal(small[:, 8 + 2 * hh:10 + 2 * hh], small[:, 4 + 2 * hh:6 + 2 * hh]))
                settled()
                nc.vector.tensor_scalar(PR[:, hh, 0:P], PR[:, hh, 0:P], small[:, 8 + 2 * hh:9 + 2 * hh], None, ALU.mult)
                nc.vector.tensor_scalar(PR[:, hh, P:384], PR[:, hh, P:384], small[:, 9 + 2 * hh:10 + 2 * hh], None, ALU.mult).then_inc(probs_ready, 1)

        def o_lo_heads(k, tile):
            for hh in range(2):
                dve.wait_ge(o_hi, k + hh + 1)
                TT(X2[:, bass.ds(tile + hh, 1), 1, :], pw[:, 2 + hh, 0:TOK].unsqueeze(1), X2[:, bass.ds(tile + hh, 1), 0, :], ALU.subtract).then_inc(o_ready, 1)

        def o_inverse_root(n):
            dve.wait_ge(o_root, n + 1)
            steps.step(nc.vector.reciprocal(rn[:, 1, :], rn[:, 0, :]))
            settled()

        def o_lo_pair(k, tile):
            dve.wait_ge(o_hi, k + 1)
            TT(X2[:, bass.ds(tile, 2), 1, :], MX[:, 0:2, :], X2[:, bass.ds(tile, 2), 0, :], ALU.subtract).then_inc(o_ready, 1)

        def mask_tables(hh):
            return mask

        def moba(i):
            s = At("moba", i, 8, 4)

            def after(m):
                if m == 3:
                    evac(s, 0, QK[:, 0:2, :])
                if m == 7:
                    evac(s, 1, QK[:, 2:4, :])
                if m == 9:
                    rope(i)
                if m == 11:
                    logits(2 * i, 2 * i, mask_tables, SCALE)
                    evac(s, 2, V)
                    normalise(2 * i, 2 * i)
                if m == 15:
                    evac(s, 3, t[:, (s.u + 3) % 2])
                    o_lo_heads(2 * i, 2 * i)
                    dve.wait_ge(sig_done, i + 1)
            each_half(s, MIX, after)
        moba(0)
        loop(dve, steps, 4, 5, moba, start=1)

        def diff(i):
            s = At("diff", i, 8, 4)

            def combine():
                dve.wait_ge(exp_done, 2 * i + 10)
                steps.step(nc.vector.reciprocal(small[:, 8:12], small[:, 4:8]))
                settled()
                steps.step(nc.vector.tensor_scalar(small[:, 12:14], small[:, 10:12], neg_lambda, None, ALU.mult))
                steps.step(nc.vector.tensor_scalar(PR[:, 0, 0:P], PR[:, 0, 0:P], small[:, 8:9], None, ALU.mult))
                steps.step(nc.vector.tensor_scalar(PR[:, 0, P:384], PR[:, 0, P:384], small[:, 9:10], None, ALU.mult))
                settled()
                STT(PR[:, 0, 0:P], PR[:, 1, 0:P], small[:, 12:13], PR[:, 0, 0:P], ALU.mult, ALU.add)
                STT(PR[:, 0, P:384], PR[:, 1, P:384], small[:, 13:14], PR[:, 0, P:384], ALU.mult, ALU.add).then_inc(probs_ready, 1)

            def after(m):
                if m == 3:
                    evac(s, 0, QK[:, 0:2, :])
                if m == 7:
                    evac(s, 1, QK[:, 2:4, :])
                if m == 9:
                    rope(i + 4)
                if m == 11:
                    logits(2 * i + 8, 2 * i + 8, mask_tables, SCALE)
                    evac(s, 2, V)
                    combine()
                if m == 15:
                    dve.wait_ge(pv_done, 8 + i + 1)
                    nc.vector.tensor_copy(MX[:, 0:2, :], pw[:, 2:4, 0:TOK]).then_inc(o_raw, 1)
                    evac(s, 3, t[:, (s.u + 3) % 2])
                if m == 2 and not isinstance(i, int):
                    finish_diff(i - 1)
            each_half(s, MIX, after)

        def finish_diff(n):
            o_inverse_root(n)
            for j in range(2):
                ins = STT(MX[:, j, :], MX[:, j, :], g_sub_scaled[:, j:j + 1], rn[:, 1, :], ALU.mult, ALU.mult)
            ins.then_inc(o_normed, 1)
            o_lo_pair(8 + n, 8 + 2 * n)
        diff(0)
        loop(dve, steps, 4, 8, diff, start=1)

        def branch(i):
            s = At("branch", i, 8, 6)

            def after(m):
                if m == 2 and isinstance(i, int):
                    finish_diff(3)
                n = m // 8
                s0 = (s.u + 3 * n) % 2
                pair = bass.ds(4 * i + 2 * n, 2)
                if m % 8 == 3:
                    evac(s, 3 * n, t[:, s0])
                if m % 8 == 5:
                    evac(s, 3 * n + 1, t[:, 1 - s0])
                    evaced(s, 3 * n + 1)
                    steps.step(TT(G[:, pair, :], G[:, pair, :], t[:, 1 - s0], ALU.mult))
                if m % 8 == 7:
                    dve.wait_ge(sig_done, 8 + 2 * i + n + 1)
                    evac(s, 3 * n + 2, t[:, s0])
                    evaced(s, 3 * n + 2)
                    steps.step(TT(t[:, s0], t[:, s0], sg, ALU.mult))
                    settled()
                    TT(G[:, pair, :], G[:, pair, :], t[:, s0], ALU.add).then_inc(gated, 1)
                    dve.wait_ge(gated, 2 * i + n + 1)
            each_half(s, BRANCH, after)
        branch(0)
        loop(dve, steps, 4, 4, branch, start=1)
        for c in range(4):
            x1_lo(1, c)

        def out1(i):
            s = At("out1", i, 4, 2)

            def after(m):
                if m % 4 == 3:
                    u = m // 4
                    evac(s, u, G[:, bass.ds(4 * i + 2 * u, 2), :])
            each_half(s, TWO, after)
        loop(dve, steps, 4, 0, out1)
        inverse_root(1)
        post_norm(1, "g_mix_post")
        inverse_root(2)
        pre_norm(2, "g_mlp_pre")

        def ffn1(b):
            def up(i):
                s = At("ffn1", i, 4, 2, outer_turn=b * 8, outer_units=b * 16)

                def after(m):
                    if m % 4 == 3:
                        u = m // 4
                        k = b * 8 + 2 * i + u
                        tile = t[:, (s.u + u) % 2]
                        evac(s, u, tile)
                        evaced(s, u)
                        STT(tile, tile, 0.0, tile, ALU.max, ALU.mult).then_inc(hid_done, 1)
                        dve.wait_ge(hid_hi, k + 1)
                        TT(X2[:, bass.ds(4 * i + 2 * u, 2), 1, :], tile, X2[:, bass.ds(4 * i + 2 * u, 2), 0, :], ALU.subtract).then_inc(hid_ready, 1)
                each_half(s, TWO, after)

            def down(i):
                s = At("ffn1", i, 4, 2, g=16, u=8, outer_turn=b * 8, outer_units=b * 16)

                def after(m):
                    if m % 4 == 3:
                        u = m // 4
                        tile, pair = t[:, (s.u + u) % 2], bass.ds(4 * i + 2 * u, 2)
                        evac(s, u, tile)
                        evaced(s, u)
                        dve.wait_ge(tiles_done, TILES_FFN1 + b * 8 + 2 * i + u)
                        TT(G[:, pair, :], G[:, pair, :], tile, ALU.add).then_inc(tiles_done, 1)
                each_half(s, DOWN, after)
            loop(dve, steps, 4, 0, up)
            loop(dve, steps, 4, 0, down)
        loop(dve, steps, 4, 0, ffn1)

        def embed(k):
            dve.wait_ge(p_hi, k + 1)
            TT(X2[:, 0:2, 1, :], pw[:, 2, :].rearrange("p (a t) -> p a t", a=2), X2[:, 0:2, 0, :], ALU.subtract).then_inc(p_ready, 1)

        def proj_granule(at, g):
            for c in range(4):
                if c % 2 == 0:
                    lo(at, 2 * g + c // 2)
                u = 4 * g + c
                evac(at, u, E[:, 2 * u:2 * u + 2, :])

        s = At("proj1")
        embed(0)
        proj_granule(s, 0)
        inverse_root(3)
        post_norm(2, "g_mlp_post", [lambda: None, lambda: proj_granule(s, 1), lambda: None, lambda: None])
        inverse_root(4)
        pre_norm(3, "g_ple_pre")

        def gate(name, sig, gated0, dst, final=False):
            def body(i):
                s = At(name, i, 4, 2)

                def after(m):
                    if m % 4 == 3:
                        u = m // 4
                        pair = bass.ds(4 * i + 2 * u, 2)
                        evac(s, u, t[:, (s.u + u) % 2])
                        dve.wait_ge(sig_done, sig + 2 * i + u + 1)
                        if dst is G:
                            TT(G[:, pair, :], E[:, pair, :], sg, ALU.mult).then_inc(gated, 1)
                        else:
                            steps.step(TT(sg, E[:, pair, :], sg, ALU.mult))
                            settled()
                            TT(h[:, pair, :], h[:, pair, :], sg, ALU.add).then_inc(gated, 1)
                        dve.wait_ge(gated, gated0 + 2 * i + u + 1)
                each_half(s, TWO, after, final)
            return body
        loop(dve, steps, 4, 0, gate("gate1", 16, 8, G))
        inverse_root(5)
        post_norm(3, "g_ple_post")
        inverse_root(6)
        pre_norm(4, "mix_norm_g_2")

        dve.wait_ge(gate_split_hi, 1)
        TT(gate_split[:, :, 1, :], gate_w[:, :, :], gate_split[:, :, 0, :], ALU.subtract).then_inc(gate_split_lo, 1)
        dve.wait_ge(x1_ready, 20)
        steps.step(nc.vector.tensor_copy(SEL[0:16], ident[0:16, 0:16].unsqueeze(2).to_broadcast([16, 16, P])))

        def gate_steps(m):
            if m == 4:
                dve.wait_ge(gates, 2)
                TT(GR[0:16, 1], pw[0:16, 0, 0:TOK], GR[0:16, 0], ALU.add).then_inc(gates, 1)
                dve.wait_ge(gates, 3)
                nc.vector.tensor_scalar(GR[0:16, 1], GR[0:16, 1], small[0:16, 40:41], None, ALU.add).then_inc(gates, 1)
                dve.wait_ge(gates, 7)
                STT(GR[0:16, 3], GR[0:16, 1], 0.0, GR[0:16, 2], ALU.min, ALU.subtract).then_inc(gates, 1)
                for pad in pads:
                    steps.step(nc.vector.memset(pad[:, 0:P], 0.0))
            if m == 7:
                dve.wait_ge(gates, 12)
                TT(GR[0:4, 0], pw[0:4, 3, 0:TOK], GR[0:4, 4], ALU.subtract).then_inc(gates, 1)
                dve.wait_ge(gates, 13)
                steps.step(nc.vector.tensor_copy(pads[0][:, P:384], GR[0:4, 0]))
                settled()
                for k in range(8):
                    src, dst, back = pads[k % 2], pads[1 - k % 2], 1 << k
                    nc.vector.tensor_tensor(dst[:, P:384], src[:, P:384], src[:, P - back:384 - back], ALU.max).then_inc(gates, 1)
                    dve.wait_ge(gates, 14 + k)
                TT(GR[0:4, 2], GR[0:4, 4], pads[0][:, P:384], ALU.add).then_inc(gates, 1)
        pads = [GR[0:4, 5:8, :].rearrange("p a b -> p (a b)")[:, 384 * k:384 * k + 384] for k in range(2)]

        def mlstm(i):
            s = At("mlstm", i, 8, 4)
            first = isinstance(i, int)

            def after(m):
                if m == 2 and not first:
                    finish_mlstm(i - 1)
                if m == 3:
                    evac(s, 0, QK[:, 0:2, :])
                if m == 7:
                    evac(s, 1, QK[:, 2:4, :])
                if first:
                    gate_steps(m)
                if m == (13 if first else 9):
                    dve.wait_ge(wt_done, i + 1)
                    dve.wait_ge(scores_done, 17 + i)
                    STT(PT[:, 0, :], pw[:, 2, 0:384], MLSTM_SCALE, PR[:, 0, :], ALU.mult, ALU.mult).then_inc(pt_gated, 1)
                if m == 11:
                    evac(s, 2, V)
                if m == (14 if first else 13):
                    dve.wait_ge(den_abs, i + 1)
                    steps.step(TT(rn[:, 1, :].unsqueeze(1), rn[:, 0, :].unsqueeze(1), G_FLOOR[:, bass.ds(i, 1), :], ALU.max))
                    settled()
                    steps.step(nc.vector.reciprocal(rn[:, 1, :], rn[:, 1, :]))
                    settled()
                    dve.wait_ge(pv_done, 13 + i)
                    TT(MX[:, 0:2, :], pw[:, 2:4, 0:TOK], over(rn[:, 1, :], 2), ALU.mult).then_inc(o_raw, 1)
                if m == 15:
                    evac(s, 3, t[:, (s.u + 3) % 2])
            each_half(s, MIX, after)

        def finish_mlstm(n):
            o_inverse_root(n + 4)
            for j in range(2):
                steps.step(STT(MX[:, j, :], MX[:, j, :], cols[:, bass.ds(col["mlstm_out_g_2"] + j + 2 * n, 1)], rn[:, 1, :], ALU.mult, ALU.mult))
            settled()
            dve.wait_ge(sig_done, 24 + n + 1)
            TT(MX[:, 0:2, :], MX[:, 0:2, :], sg, ALU.mult).then_inc(o_normed, 1)
            o_lo_pair(12 + n, 2 * n)
        mlstm(0)
        loop(dve, steps, 4, 5, mlstm, start=1)

        def fox(i):
            s = At("fox", i, 12, 6)

            def norm_qk(q):
                dve.wait_ge(qk_root, q + 1)
                steps.step(nc.vector.reciprocal(MX, MX))
                settled()
                steps.step(STT(QK[:, 0:2, :], QK[:, 0:2, :], gq_scaled, MX[:, 0:2, :], ALU.mult, ALU.mult))
                STT(QK[:, 2:4, :], QK[:, 2:4, :], vec("fox_k_g_2", 0), MX[:, 2:4, :], ALU.mult, ALU.mult).then_inc(qk_ready, 1)

            def decay_tables(q):
                def table(hh):
                    dve.wait_ge(bias_done, 2 * q + hh + 1)
                    return DK[:, hh]
                return table

            def after(m):
                r = m // 12
                q = 2 * i + r
                if m % 12 == 3:
                    evac(s, 3 * r, QK[:, 0:2, :])
                if m % 12 == 7:
                    evac(s, 3 * r + 1, QK[:, 2:4, :])
                if m % 12 == 9:
                    norm_qk(q)
                if m % 12 == 11:
                    evac(s, 3 * r + 2, V)
                if m in (12, 23):
                    k = i * 4 + (2 if m == 23 else 0)
                    logits(20 + k, 16 + k, decay_tables(i * 2 + (1 if m == 23 else 0)), 1.0)
                    normalise(16 + k, 12 + k)
                if m == 16:
                    o_lo_heads(16 + 4 * i, 8 + 4 * i)
                if m == 2:
                    finish_mlstm(3) if i == 0 else finish_fox(0)
            each_half(s, FOX, after)

        def finish_fox(j):
            o_lo_heads(18 + 4 * j, 10 + 4 * j)
        fox(0)
        fox(1)

        def add_h(name, tiles, rows, g=0, u=0, outer_tiles=0, **outer):
            def body(i):
                s = At(name, i, 4, 2, g=g, u=u, **outer)

                def after(m):
                    if m == 2 and name == "out2" and isinstance(i, int):
                        finish_fox(1)
                    if m % 4 == 3:
                        uu = m // 4
                        tile, pair = t[:, (s.u + uu) % 2], bass.ds(4 * i + 2 * uu, 2)
                        evac(s, uu, tile)
                        evaced(s, uu)
                        dve.wait_ge(tiles_done, tiles + 2 * i + uu + outer_tiles)
                        TT(h[:, pair, :], h[:, pair, :], tile, ALU.add).then_inc(tiles_done, 1)
                each_half(s, rows, after)
            return body
        add_h("out2", TILES_OUT2, TWO)(0)
        loop(dve, steps, 4, 0, add_h("out2", TILES_OUT2, TWO), start=1)
        dve.wait_ge(tiles_done, TILES_OUT2 + 8)
        steps.step(nc.vector.memset(a_pad[:, :, 0:2], 0.0))
        inverse_root(7)
        pre_norm(5, "ffn_norm_g_2")

        def ffn2(name, b, pairs, k0):
            turn, units = (b * 12, b * 24) if name == "ffn2" else (0, 0)
            tile0 = b * 16 if name == "ffn2" else 32

            def up(i):
                s = At(name, i, 4, 2, outer_turn=turn, outer_units=units)

                def tap(w, j):
                    return cols[:, bass.ds(CONV + w * FFT2 + j + tile0 + 2 * i, 1)]

                def after(m):
                    if m == 3:
                        evac(s, 0, a_pad[:, :, 2:TOK + 2])
                        evaced(s, 0)
                        tile = t[:, s.u % 2]
                        for j in range(2):
                            steps.step(nc.vector.tensor_scalar(tile[:, j, :], a_pad[:, j, 0:TOK], tap(0, j), None, ALU.mult))
                        settled()
                        for j in range(2):
                            steps.step(STT(tile[:, j, :], a_pad[:, j, 1:TOK + 1], tap(1, j), tile[:, j, :], ALU.mult, ALU.add))
                        settled()
                        for j in range(2):
                            ins = STT(tile[:, j, :], a_pad[:, j, 2:TOK + 2], tap(2, j), tile[:, j, :], ALU.mult, ALU.add)
                        ins.then_inc(conv_done, 1)
                    if m == 7:
                        tile = t[:, (s.u + 1) % 2]
                        evac(s, 1, tile)
                        evaced(s, 1)
                        dve.wait_ge(sig_done, 28 + k0 + i + 1)
                        TT(tile, tile, sg, ALU.mult).then_inc(hid_done, 1)
                        dve.wait_ge(hid_hi, 32 + k0 + i + 1)
                        TT(X2[:, bass.ds(2 * i, 2), 1, :], tile, X2[:, bass.ds(2 * i, 2), 0, :], ALU.subtract).then_inc(hid_ready, 1)
                each_half(s, TWO, after)
            loop(dve, steps, pairs, 4, up)
            rows = DOWN if name == "ffn2" else DOWN3
            ot = b * 8 if name == "ffn2" else 16
            loop(dve, steps, 4, 0, add_h(name, TILES_FFN2, rows, 4 * pairs, 2 * pairs, outer_tiles=ot, outer_turn=turn, outer_units=units))
        loop(dve, steps, 2, 32, lambda b: ffn2("ffn2", b, 8, b * 8))
        ffn2("ffn2b", 0, 6, 16)
        dve.wait_ge(tiles_done, TILES_FFN2 + 24)

        s2 = At("proj2")
        embed(1)
        proj_granule(s2, 0)
        inverse_root(8)
        pre_norm(6, "ple_norm_g_2", [lambda: None, lambda: proj_granule(s2, 1), lambda: None, lambda: None])
        loop(dve, steps, 3, 2, gate("gate2", 50, 16, h))
        gate("gate2", 50, 16, h, final=True)(3)

    @block.tensor
    def _(pe):
        MM, T = nc.tensor.matmul, nc.tensor.transpose

        def unit_start(at, u):
            k = at.unit(u) - 1
            if not (isinstance(k, int) and k <= 0):
                pe.wait_ge(evac_done, k)

        def blocks(at, m, u, form, op, b0, tiles, first, last):
            slot = (2 * at.g + m) % RING
            s = (at.u + u) % 2
            for n, kt in enumerate(tiles):
                w = split[:, slot, b0 + n]
                start, stop = first and n == 0, last and n == len(tiles) - 1
                for j in range(2):
                    bank, js = 2 * s + j, slice(j * P, j * P + P)
                    if form == "features":
                        stay_hi, stay_lo, move = w[:, 0, js], w[:, 1, js], op[:, kt]
                    else:
                        stay_hi, stay_lo, move = op[:, kt, 0, js], op[:, kt, 1, js], w
                    MM(ps[:, bank, :], stay_hi, move, start=start, stop=False, skip_group_check=True)
                    ins = MM(ps[:, bank, 0:TOK], stay_lo, move[:, 0, :], start=False, stop=stop, skip_group_check=True)
            return ins

        def each_half(at, rows, ready=None, before=None):
            for m, (u, form, op, k0, per, first, last) in enumerate(rows):
                if before:
                    before(m)
                if first:
                    unit_start(at, u)
                if ready:
                    ready(m, u, k0)
                pe.wait_ge(lo_done, at.halves(m) + 1)
                blocks(at, m, u, form, op, 0, range(k0, k0 + per), first, last).then_inc(half_used, 1)

        def x1_is(e):
            def ready(m, u, k0):
                if u == 0:
                    pe.wait_ge(x1_ready, 4 * e + k0 // 4 + 1)
            return ready

        def sum_acc(k):
            pe.wait_ge(unit_squares, 8 * k + 8)
            MM(pw[:, 0, 0:TOK], ones, acc[:, 0, :], start=True, stop=False)
            MM(pw[:, 0, 0:TOK], ones, acc[:, 1, :], start=False, stop=True).then_inc(sums_done, 1)

        def sum_tiles(k):
            for kt in range(KT):
                if kt % 4 == 0:
                    pe.wait_ge(squares_ready, 4 * k + kt // 4 + 1)
                ins = MM(pw[:, 0, 0:TOK], ones, G[:, kt, :], start=kt == 0, stop=kt == KT - 1)
            ins.then_inc(sums_done, 1)

        pe.wait_ge(const_landed, 16)
        pe.wait_ge(x_landed, 16)
        for b in range(8):
            if b >= 4 and b % 2 == 0:
                pe.wait_ge(h_ready, b // 2 - 1)
            for f in range(2):
                for q in range(2):
                    kt = 2 * b + f
                    ins = T(pw[:, b % 4, f * TOK + q * P:f * TOK + q * P + P], x_rows[:, q, kt * P:kt * P + P], ident)
            ins.then_inc(x_turned, 1)
        pe.wait_ge(vec_landed, 16 * 21)
        pe.wait_ge(h_ready, 3)
        T(pw[:, 0, 0:P], vec_rows[:, 0, :], ident)
        T(pw[:, 0, P:P + n_rows2], vec_rows[0:n_rows2, 1, :], ident[0:n_rows2, 0:n_rows2])
        T(pw[:, 1, 0:2 * FFT2], vec_rows[0:2 * FFT2, 2, :], ident[0:2 * FFT2, 0:2 * FFT2])
        T(pw[:, 1, 2 * FFT2:4 * FFT2], vec_rows[0:2 * FFT2, 3, :], ident[0:2 * FFT2, 0:2 * FFT2]).then_inc(vec_turned, 1)
        pe.wait_ge(vec_copied, 2)
        sum_tiles(0)
        pe.wait_ge(lam_parts, 1)
        MM(pw[:, 1, 0:2], ones, small[:, 20:22], start=True, stop=True).then_inc(lam_summed, 1)

        def rotate(at, p):
            pe.wait_ge(evac_done, at.unit(1) + 1)
            for c in range(2):
                ins = MM(pw[:, c, :], rot, QK[0:32, 2 * c:2 * c + 2, :], start=True, stop=True)
            ins.then_inc(rot_done, 1)

        def score(k):
            for hh in range(2):
                MM(pw[:, 2 + hh, 0:P], QK[:, hh, 0:P], QK[:, 2 + hh, 0:P], start=True, stop=True)
                MM(pw[:, 2 + hh, P:384], QK[:, hh, P:TOK], QK[:, 2 + hh, :], start=True, stop=True).then_inc(scores_done, 1)

        def turn_probs(k, heads):
            for hh in range(heads):
                pe.wait_ge(probs_ready, k + hh + 1)
                for b in range(3):
                    ins = T(pw[:, hh, b * P:b * P + P], PR[:, hh, b * P:b * P + P], ident)
                ins.then_inc(probs_turned, 1)

        def weigh(bank, values, pt):
            MM(pw[:, bank, 0:TOK], values(0), pt[:, 0:TOK], start=True, stop=False, skip_group_check=True)
            return MM(pw[:, bank, P:TOK], values(1), pt[:, TOK:384], start=False, stop=True, skip_group_check=True)

        def weigh_heads(at, u, k):
            pe.wait_ge(evac_done, at.unit(u) + 1)
            for hh in range(2):
                pe.wait_ge(pt_ready, k + hh + 1)
                weigh(2 + hh, lambda key, hh=hh: V[:, key, hh * P:hh * P + P], PT[:, hh]).then_inc(pv_done, 1)

        def weigh_tiles():
            for j in range(2):
                ins = weigh(2 + j, lambda key, j=j: V[:, key, j * P:j * P + P], PT[:, 0])
            ins.then_inc(pv_done, 1)

        def sum_o(n):
            pe.wait_ge(o_squares, n + 1)
            MM(pw[:, 1, 0:TOK], ones, MX[:, 2, :], start=True, stop=False)
            MM(pw[:, 1, 0:TOK], ones, MX[:, 3, :], start=False, stop=True).then_inc(o_sums, 1)

        def moba(i):
            s = At("moba", i, 8, 4)

            def before(m):
                if m == 9:
                    rotate(s, i)
                if m == 11:
                    pe.wait_ge(rope_done, i + 1)
                    if not isinstance(i, int):
                        pe.wait_ge(o_ready, 2 * i)
                    score(2 * i)
                if m == 13:
                    turn_probs(2 * i, 2)
                if m == 15:
                    weigh_heads(s, 2, 2 * i)
            each_half(s, MIX, x1_is(0), before)
        moba(0)
        loop(pe, Chain(None), 4, 0, moba, start=1)

        def diff(i):
            s = At("diff", i, 8, 4)

            def before(m):
                if m == 9:
                    pe.wait_ge(o_ready, 8 + i)
                    rotate(s, i + 4)
                if m == 11:
                    pe.wait_ge(rope_done, i + 5)
                    pe.wait_ge(o_ready, 8 + i)
                    score(2 * i + 8)
                if m == 13:
                    turn_probs(8 + i, 1)
                if m == 15:
                    pe.wait_ge(evac_done, s.unit(2) + 1)
                    pe.wait_ge(pt_ready, 8 + i + 1)
                    weigh_tiles()
                if m == 2 and not isinstance(i, int):
                    sum_o(i - 1)
            each_half(s, MIX, None, before)
        diff(0)
        loop(pe, Chain(None), 4, 0, diff, start=1)

        def finish_diff(m):
            if m == 2:
                sum_o(3)
            if m == 4:
                pe.wait_ge(o_ready, 12)
        each_half(At("branch"), BRANCH, None, finish_diff)
        loop(pe, Chain(None), 4, 0, lambda i: each_half(At("branch", i, 8, 6), BRANCH), start=1)
        loop(pe, Chain(None), 4, 0, lambda i: each_half(At("out1", i, 4, 2), TWO, x1_is(1)))
        sum_acc(0)
        sum_tiles(1)

        def ffn1(b):
            outer = dict(outer_turn=b * 8, outer_units=b * 16)

            def hidden(m, u, k0):
                if u == 0:
                    pe.wait_ge(hid_ready, b * 8 + k0 // 2 + 2)
            loop(pe, Chain(None), 4, 0, lambda i: each_half(At("ffn1", i, 4, 2, **outer), TWO, x1_is(2)))
            loop(pe, Chain(None), 4, 0, lambda i: each_half(At("ffn1", i, 4, 2, g=16, u=8, **outer), DOWN, hidden))
        loop(pe, Chain(None), 4, 0, ffn1)

        def embed(k):
            pe.wait_ge(p_landed, 16 * (k + 1))
            for f in range(2):
                for q in range(2):
                    ins = T(pw[:, 2, f * TOK + q * P:f * TOK + q * P + P], emb[:, q, f * P:f * P + P], ident)
            ins.then_inc(p_turned, 1)

        def proj_granule(at, g):
            pe.wait_ge(lo_done, at.halves(2 * g) + 2)
            for c in range(4):
                u = 4 * g + c
                unit_start(at, u)
                first = blocks(at, 2 * g, u, "features", X2, c, range(1), True, False)
                last = blocks(at, 2 * g + 1, u, "features", X2, c, range(1, 2), False, True)
                if c < 3:
                    last.then_inc(pair_used, 1)
                else:
                    first.then_inc(half_used, 1)
                    last.then_inc(half_used, 1)

        s = At("proj1")
        embed(0)
        pe.wait_ge(p_ready, 1)
        proj_granule(s, 0)
        sum_acc(1)
        proj_granule(s, 1)
        sum_tiles(2)
        loop(pe, Chain(None), 4, 0, lambda i: each_half(At("gate1", i, 4, 2), TWO, x1_is(3)))
        sum_acc(2)
        sum_tiles(3)

        def gate_steps(m):
            if m == 4:
                pe.wait_ge(gate_split_lo, 1)
                for kt in range(KT):
                    MM(pw[0:16, 0, :], gate_split[:, kt, 0, :], X1[:, kt], start=kt == 0, stop=False, skip_group_check=True)
                    ins = MM(pw[0:16, 0, 0:TOK], gate_split[:, kt, 1, :], X1[:, kt, 0, :], start=False, stop=kt == KT - 1, skip_group_check=True)
                ins.then_inc(gates, 1)
            if m == 7:
                pe.wait_ge(gates, 8)
                for q in range(2):
                    ins = T(pw[:, 1, 16 * q:16 * q + 16], GR[0:16, 3, q * P:q * P + P], ident[0:16, 0:16])
                ins.then_inc(gates, 1)
            if m == 8:
                pe.wait_ge(gates, 10)
                MM(pw[0:16, 2, 0:TOK], small[:, 0:16], tri, start=True, stop=False, skip_group_check=True)
                MM(pw[0:16, 2, P:TOK], small[:, 16:32], tri[:, 0:P], start=False, stop=True, skip_group_check=True)
                MM(pw[0:4, 3, 0:TOK], ident[0:16, 12:16], GR[0:16, 1], start=True, stop=True).then_inc(gates, 1)
            if m == 10:
                pe.wait_ge(gates, 23)
                for q in range(2):
                    ins = T(pw[:, 0, 4 * q:4 * q + 4], GR[0:4, 0, q * P:q * P + P], ident[0:4, 0:4])
                ins.then_inc(gates, 1)
            if m == 11:
                pe.wait_ge(gates, 25)
                top = GR[0:4, 5:8, :].rearrange("p a b -> p (a b)")[:, P:384]
                for r in range(4):
                    MM(pw[:, r // 2, (r % 2) * TOK:(r % 2) * TOK + TOK], SEL[0:4, r, :], top, start=True, stop=True)
                    ins = MM(pw[:, 2 + r // 2, (r % 2) * TOK:(r % 2) * TOK + TOK], SEL[0:4, r, :], GR[0:4, 3], start=True, stop=True)
                ins.then_inc(gates, 1)
            if m == 12:
                pe.wait_ge(gates, 28)
                for r in range(8):
                    ins = MM(pw[:, r // 2, (r % 2) * TOK:(r % 2) * TOK + TOK], SEL[0:16, 4 + r, :], GR[0:16, 4], start=True, stop=True)
                ins.then_inc(gates, 1)
            if m == 13:
                pe.wait_ge(gates, 30)

        def mlstm(i):
            s = At("mlstm", i, 8, 4)
            first = isinstance(i, int)

            def before(m):
                if first:
                    gate_steps(m)
                elif m == 2:
                    sum_o(i - 1 + 4)
                if m == (13 if first else 9):
                    pe.wait_ge(evac_done, s.unit(1) + 1)
                    pe.wait_ge(o_raw, i + 4)
                    for q, (a0, a1, t0) in enumerate(((0, TOK, 0), (TOK, 384, P))):
                        for c in range(2):
                            ins = MM(pw[:, 2, a0:a1], QK[:, 2 + c, q * P:q * P + P], QK[:, c, t0:TOK], start=c == 0, stop=c == 1)
                    ins.then_inc(scores_done, 1)
                if m == (15 if first else 13):
                    pe.wait_ge(pt_gated, i + 1)
                    pe.wait_ge(evac_done, s.unit(2) + 1)
                    weigh(1, lambda key: ones, PT[:, 0]).then_inc(den_done, 1)
                    weigh_tiles()
            each_half(s, MIX, x1_is(4), before)
        mlstm(0)
        loop(pe, Chain(None), 4, 0, mlstm, start=1)

        def fox(i):
            s = At("fox", i, 12, 6)

            def sum_qk(q):
                pe.wait_ge(qk_squares, q + 1)
                for c in range(2):
                    ins = MM(pw[:, c, :], ones, MX[:, 2 * c:2 * c + 2, :], start=True, stop=True)
                ins.then_inc(qk_sums, 1)

            def before(m):
                if m in (9, 21):
                    sum_qk(2 * i + m // 12)
                if m == 12:
                    pe.wait_ge(qk_ready, 2 * i + 1)
                    pe.wait_ge(o_ready, 16 + 4 * i)
                    score(20 + 4 * i)
                if m == 14:
                    turn_probs(12 + 4 * i, 2)
                if m == 16:
                    weigh_heads(s, 2, 12 + 4 * i)
                if m == 23:
                    pe.wait_ge(qk_ready, 2 * i + 2)
                    pe.wait_ge(o_ready, 18 + 4 * i)
                    score(22 + 4 * i)
                if i == 0 and m == 2:
                    sum_o(7)
                if i == 1:
                    finish_fox(s, 0, m)
            each_half(s, FOX, None, before)

        def finish_fox(at, j, m):
            if m == 1:
                turn_probs(14 + 4 * j, 2)
            if m == 2:
                weigh_heads(at, -1, 14 + 4 * j)
        fox(0)
        fox(1)

        def finish_last(m):
            finish_fox(At("out2"), 1, m)
            if m == 3:
                pe.wait_ge(o_ready, 24)
        each_half(At("out2"), OUT2, None, finish_last)
        loop(pe, Chain(None), 4, 0, lambda i: each_half(At("out2", i, 4, 2), OUT2), start=1)
        sum_acc(3)

        def ffn2(name, b, pairs, k0):
            outer = dict(outer_turn=b * 12, outer_units=b * 24) if name == "ffn2" else {}

            def hidden(m, u, tile):
                if u == 0:
                    pe.wait_ge(hid_ready, 32 + k0 + min(tile // 2 + 2, pairs))
            loop(pe, Chain(None), pairs, 0, lambda i: each_half(At(name, i, 4, 2, **outer), TWO, x1_is(5)))
            loop(pe, Chain(None), 4, 0, lambda i: each_half(At(name, i, 4, 2, g=4 * pairs, u=2 * pairs, **outer), DOWN if name == "ffn2" else DOWN3, hidden))
        loop(pe, Chain(None), 2, 0, lambda b: ffn2("ffn2", b, 8, b * 8))
        ffn2("ffn2b", 0, 6, 16)

        s2 = At("proj2")
        embed(1)
        pe.wait_ge(p_ready, 2)
        proj_granule(s2, 0)
        sum_acc(4)
        proj_granule(s2, 1)
        loop(pe, Chain(None), 4, 0, lambda i: each_half(At("gate2", i, 4, 2), TWO, x1_is(6)))
        pe.wait_ge(gated, 24)
        for k in range(8):
            if k >= 4:
                pe.wait_ge(out_copied, k - 3)
            for f in range(4):
                kt = 4 * (k % 4) + f
                ins = T(pw[:, k % 4, f * P:f * P + P], h[:, kt, (k // 4) * P:(k // 4) * P + P], ident)
            ins.then_inc(out_turned, 1)

    ctx.close()


def kernel(**inputs):
    import concourse.bacc as bacc
    from concourse.bass_utils import run_bass_kernel_spmd

    nc = bacc.Bacc("TRN2", target_bir_lowering=False, num_devices=1)
    arrays = {name: np.ascontiguousarray(inputs[name]) for name in INPUTS}
    arrays["constants"] = CONSTANTS
    aps = {n: nc.dram_tensor(f"in_{n}", v.shape, F32, kind="ExternalInput").ap() for n, v in arrays.items()}
    out = nc.dram_tensor("out", (1, TOK, DM), F32, kind="ExternalOutput").ap()
    two_blocks(nc, aps, out)
    r = run_bass_kernel_spmd(nc, [{f"in_{n}": v for n, v in arrays.items()}], core_ids=[0])
    return r.results[0]["out"]
```

```python
from contextlib import ExitStack

import numpy as np

import concourse.bass as bass
from concourse import mybir

F32 = mybir.dt.float32
F32R = mybir.dt.float32r
ALU = mybir.AluOpType
ACT = mybir.ActivationFunctionType
AX = mybir.AxisListType

P = 128
TOK = 256
DM = 2048
KT = DM // P
COL = 256
RING = 4
HALF = 4
LEAD = 3
HEADS1 = 8
FF1 = 8192
FF2 = 5632
FFT2 = FF2 // P
EPS = 1e-6
LAMBDA_INIT = 0.2
SCALE = 128 ** -0.5
MLSTM_SCALE = 256 ** -0.5
MASKED = -1e30

CONST_COLS = {}


def constants():
    parts, at = [], 0

    def put(name, a):
        nonlocal at
        full = np.zeros((P, a.shape[1]), np.float32)
        full[: a.shape[0]] = a
        CONST_COLS[name] = (at, at + a.shape[1])
        at += a.shape[1]
        parts.append(full)

    r = np.arange(P)
    put("ident", np.eye(P, dtype=np.float32))
    diag = np.where(r[None, :] <= r[:, None], 0.0, MASKED).astype(np.float32)
    put("mask", np.concatenate([diag, np.zeros((P, P), np.float32), diag], 1))
    put("mask_t", np.concatenate([diag.T, np.zeros((P, P), np.float32), diag.T], 1))
    upper = (r[:, None] <= r[None, :]).astype(np.float32)
    put("tri_ones", np.concatenate([upper, np.ones((P, P), np.float32)], 1))
    rot_dim = 32
    half = rot_dim // 2
    inv = (np.float32(1.0) / (np.float32(500000.0) ** (np.arange(half, dtype=np.float32) * np.float32(2.0) / np.float32(rot_dim)))).astype(np.float32)
    ang = (np.arange(TOK, dtype=np.float32)[None, :] * inv[:, None]).astype(np.float32).astype(np.float64)
    put("cos", np.tile(np.cos(ang), (2, 1)).astype(np.float32))
    put("sin", np.tile(np.sin(ang), (2, 1)).astype(np.float32))
    rot = np.zeros((rot_dim, P), np.float32)
    for m in range(half):
        rot[m + half, m] = -1.0
        rot[m, m + half] = 1.0
    put("rot", rot)
    return np.concatenate(parts, 1)


CONSTANTS = constants()
NCONST = CONSTANTS.shape[1]

PHASES = [
    ("moba", 4, 8, 4), ("diff", 4, 8, 4), ("branch", 4, 8, 6), ("out1", 4, 4, 2),
    ("ffn1", 4, 32, 16), ("proj1", 1, 2, 8), ("gate1", 4, 4, 2),
    ("mlstm", 4, 8, 4), ("fox", 2, 12, 6), ("out2", 4, 4, 2),
    ("ffn2", 2, 48, 24), ("ffn2b", 1, 40, 20), ("proj2", 1, 2, 8), ("gate2", 4, 4, 2),
]
G0, U0 = {}, {}
_g = _u = 0
for _name, _n, _pg, _pu in PHASES:
    G0[_name], U0[_name] = _g, _u
    _g += _n * _pg
    _u += _n * _pu
GRANULES = _g


class At:

    def __init__(self, name, i=0, per_g=0, per_u=0, g=0, u=0, outer_turn=0, outer_units=0):
        self.g, self.u = G0[name] + g, U0[name] + u
        self.turn = i * (per_g // RING) + outer_turn
        self.units = i * per_u + outer_units

    def halves(self, m):
        return 2 * self.g + m + 2 * RING * self.turn

    def unit(self, u):
        return self.u + u + self.units


class Chain:

    def __init__(self, sem):
        self.sem, self.n, self.dyn = sem, 0, 0

    def step(self, ins):
        ins.then_inc(self.sem, 1)
        self.n += 1

    def done(self):
        return self.n + self.dyn


def loop(eng, chain, count, steps, body, start=0):
    first, outer = chain.n, chain.dyn
    with eng.Fori(start, count) as i:
        chain.dyn = outer + (i - start) * steps if steps else outer
        body(i)
    assert chain.n - first == steps, (eng, chain.n - first, steps)
    chain.n = first + (count - start) * steps
    chain.dyn = outer


INPUTS = [
    "x", "p", "w_in", "w_br_moba", "w_br_diff", "w_out", "lambda_q1", "lambda_k1", "lambda_q2", "lambda_k2",
    "diff_subln_g", "g_mix_pre", "g_mix_post", "w_up", "w_down", "g_mlp_pre", "g_mlp_post", "w_ple_proj",
    "w_ple_gate", "g_ple_pre", "g_ple_post", "p_2", "mix_norm_g_2", "w_in_2", "mlstm_gate_bias_2",
    "mlstm_out_g_2", "fox_q_g_2", "fox_k_g_2", "fox_f_bias_2", "w_out_2", "ffn_norm_g_2", "w_up_2", "conv_w_2",
    "conv_b_2", "w_down_2", "ple_norm_g_2", "w_ple_gate_2", "w_ple_proj_2",
]


def over(ap, n):
    return ap.unsqueeze(1).to_broadcast([ap.shape[0], n, ap.shape[1]])


def two_blocks(nc, a, out):
    ctx = ExitStack()

    def sb(name, shape, dt=F32):
        return ctx.enter_context(nc.sbuf_tensor(name, shape, dt))

    def sem(name):
        return ctx.enter_context(nc.semaphore(name))

    raw = sb("raw", [P, RING, 2 * HALF, COL])
    split = sb("split", [P, RING, HALF, 2, COL], F32R)
    h = sb("h", [P, KT, TOK])
    X1 = sb("X1", [P, KT, 2, TOK], F32R)
    X2 = sb("X2", [P, KT, 2, TOK], F32R)
    G = sb("G", [P, KT, TOK])
    E = sb("E", [P, KT, TOK])
    cross = sb("cross", [P, 2, 2, TOK])
    t = sb("t", [P, 2, 2, TOK])
    sg = sb("sg", [P, 2, TOK])[:, :, :]
    con = sb("con", [P, NCONST])
    cols = sb("cols", [P, P + 32 + 4 * FFT2])
    small = sb("small", [P, 64])
    emb = E[:, 14:16, :]
    a_pad = E[:, 0:3, :].rearrange("p a b -> p (a b)")[:, 0:2 * (TOK + 2)].rearrange("p (j t) -> p j t", j=2)
    DK = G[:, 0:3, :].rearrange("p a b -> p (a b)").rearrange("p (h s) -> p h s", h=2)
    acc = sb("acc", [P, 2, TOK])
    rn = sb("rn", [P, 2, TOK])
    mix_rn = acc[:, 0, :]
    rn_col = small[:, 61:63]
    sq = rn
    gate_w = sg[:, 0, :].rearrange("p (k c) -> p k c", k=KT)
    gate_split = sb("gate_split", [P, KT, 2, 16], F32R)
    QK = E[:, 0:4, :]
    V = E[:, 4:6, :]
    PR = E[:, 6:9, :].rearrange("p a b -> p (a b)").rearrange("p (h s) -> p h s", h=2)
    PT = E[:, 9:12, :].rearrange("p a b -> p (a b)").rearrange("p (h s) -> p h s", h=2)
    MX = E[:, 12:16, :]
    vec_rows = E[:, 12:14, :].rearrange("p a (b c) -> p (a b) c", b=2)
    x_rows = G[:, :, :].rearrange("p k t -> p (k t)").rearrange("p (a d) -> p a d", a=2)
    out_rows = x_rows
    G_MAX, G_FLOOR, G_DECAY = G[:, 0:4, :], G[:, 4:8, :], G[:, 8:16, :]

    def const(name, rows=P):
        lo, hi = CONST_COLS[name]
        return con[0:rows, lo:hi]

    ident, mask, mask_t, tri = (const(n) for n in ("ident", "mask", "mask_t", "tri_ones"))
    ones = tri[:, P:TOK]
    rope_cos, rope_sin, rot = (const(n, 32) for n in ("cos", "sin", "rot"))

    assert CONST_COLS["sin"][0] == CONST_COLS["cos"][1]
    sq_gate = con[:, CONST_COLS["cos"][0]:CONST_COLS["sin"][1]].rearrange("p (a t) -> p a t", a=2)

    ps = ctx.enter_context(nc.psum_tensor("ps", [P, 4, 512], F32))
    pw = ctx.enter_context(nc.psum_tensor("pw", [P, 4, 512], F32))

    vectors1 = ["g_mix_pre", "g_mix_post", "g_mlp_pre", "g_mlp_post", "g_ple_pre", "g_ple_post",
                "mix_norm_g_2", "ffn_norm_g_2"]
    col = {n: 16 * k for k, n in enumerate(vectors1)}
    vectors2 = ["ple_norm_g_2", "mlstm_out_g_2", "diff_subln_g", "fox_q_g_2", "fox_k_g_2",
                "lambda_q1", "lambda_k1", "lambda_q2", "lambda_k2"]
    n_rows2 = 0
    for n in vectors2:
        col[n] = P + n_rows2
        n_rows2 += a[n].shape[-1] // P
    assert n_rows2 == 32
    CONV = P + 32
    CONV_BIAS = CONV + 3 * FFT2
    eps_col, neg_lambda, gq_scaled, g_sub_scaled = small[:, 60:61], small[:, 24:25], small[:, 57:58], small[:, 58:60]
    GR = E[:, 8:16, :]
    SEL = G[:, 8:16, :].rearrange("p a b -> p (a b)").rearrange("p (r c) -> p r c", r=16)
    TILES_FFN1, TILES_OUT2, TILES_FFN2 = 1, 33, 41
    GATE_STEPS = 30

    def vec(name, k):
        c = col[name]
        return cols[:, bass.ds(c + k, 1)]

    raw_landed = [sem(f"raw_landed{k}") for k in range(RING)]
    const_landed, x_landed, vec_landed, p_landed = (sem(n) for n in ("const_landed", "x_landed", "vec_landed", "p_landed"))
    gain_landed, rn_turned, rn_col_done = sem("gain_landed"), sem("rn_turned"), sem("rn_col_done")
    gate_w_landed = sem("gate_w_landed")
    pair_used = sem("pair_used")
    hi_done, lo_done, half_used = sem("hi_done"), sem("lo_done"), sem("half_used")
    cross_done, evac_done = sem("cross_done"), sem("evac_done")
    vec_turned, vec_copied = sem("vec_turned"), sem("vec_copied")
    x_turned, eps_ready = sem("x_turned"), sem("eps_ready")
    p_turned, p_hi, p_ready = sem("p_turned"), sem("p_hi"), sem("p_ready")
    lam_parts, lam_summed, lam_exps, lam_ready = (sem(n) for n in ("lam_parts", "lam_summed", "lam_exps", "lam_ready"))
    sums_done, root_done, rn_ready = sem("sums_done"), sem("root_done"), sem("rn_ready")
    h_ready, squares_ready = sem("h_ready"), sem("squares_ready")
    normed, x1_hi, x1_ready = sem("normed"), sem("x1_hi"), sem("x1_ready")
    rot_done, rope_cos_done, rope_done = sem("rot_done"), sem("rope_cos_done"), sem("rope_done")
    scores_done, logits_done, exp_done, probs_ready = (sem(n) for n in ("scores_done", "logits_done", "exp_done", "probs_ready"))
    probs_turned, pt_ready, pv_done = sem("probs_turned"), sem("pt_ready"), sem("pv_done")
    o_raw, o_squares, o_sums, o_root, o_normed, o_hi, o_ready = (sem(n) for n in ("o_raw", "o_squares", "o_sums", "o_root", "o_normed", "o_hi", "o_ready"))
    sig_done, gated, unit_squares, tiles_done = (sem(n) for n in ("sig_done", "gated", "unit_squares", "tiles_done"))
    conv_done, hid_done, hid_hi, hid_ready = (sem(n) for n in ("conv_done", "hid_done", "hid_hi", "hid_ready"))
    gates, gate_split_hi, gate_split_lo = sem("gates"), sem("gate_split_hi"), sem("gate_split_lo")
    wt_arg, wt_done, pt_gated, den_done, den_abs, bias_done = (sem(n) for n in ("wt_arg", "wt_done", "pt_gated", "den_done", "den_abs", "bias_done"))
    qk_squares, qk_sums, qk_root, qk_ready = (sem(n) for n in ("qk_squares", "qk_sums", "qk_root", "qk_ready"))
    out_turned, out_copied, out_landed = sem("out_turned"), sem("out_copied"), sem("out_landed")
    act_steps, dve_steps, pool_steps = sem("act_steps"), sem("dve_steps"), sem("pool_steps")

    def plan(units):
        rows = []
        for u, (form, op, k0, counts) in enumerate(units):
            for q, n in enumerate(counts):
                rows.append((u, form, op, k0 + sum(counts[:q]), n, q == 0, q == len(counts) - 1))
        return rows

    full1 = ("features", X1, 0, (4, 4, 4, 4))
    tokens1 = ("tokens", X1, 0, (4, 4, 4, 4))
    full2 = ("features", X2, 0, (4, 4, 4, 4))
    MIX = plan([full1, full1, tokens1, full1])
    BRANCH = plan(2 * [full1, ("features", X2, 0, (4, 4)), ("features", X2, 8, (4, 4))])
    TWO = plan([full1, full1])
    OUT2 = DOWN = plan([full2, full2])
    DOWN3 = plan(2 * [("features", X2, 0, (4, 2, 4, 2))])
    FOX = plan(2 * [full1, full1, tokens1])

    block = ctx.enter_context(nc.Block())

    @block.sync
    def _(sp):
        def load(at, g, source):
            k = at.g + g
            if not (isinstance(at.turn, int) and k + RING * at.turn < RING):
                sp.wait_ge(lo_done, at.halves(2 * g) - 2 * RING + 2)
            tiles = source.shape[0] // P
            dst = raw[:, k % RING, :, :].rearrange("p k c -> p (k c)")[:, 0:tiles * source.shape[1]]
            sp.dma_start(dst.rearrange("p (k c) -> p k c", k=tiles),
                         source.rearrange("(k p) c -> p k c", p=P)).then_inc(raw_landed[k % RING], 16)

        def unit(at, g, w, col0, row0=0, rows=2048):
            step = rows // 2 if rows >= 1536 else rows
            for q in range(rows // step):
                load(at, g + q, w[bass.ds(row0 + q * step, step), bass.ds(col0, COL)])

        w_in, w_in2 = a["w_in"][0], a["w_in_2"][0]

        def moba(i):
            s = At("moba", i, 8, 4)
            for u, c in enumerate((0, 1024, 2048, 6144)):
                unit(s, 2 * u, w_in, c + i * COL)

        sp.dma_start(con[:, :], a["constants"]).then_inc(const_landed, 16)
        sp.dma_start(x_rows, a["x"][0].rearrange("(a p) d -> p a d", p=P)).then_inc(x_landed, 16)
        moba(0)
        loop(sp, Chain(None), 4, 0, moba, start=1)

        def diff(i):
            s = At("diff", i, 8, 4)
            for u, c in enumerate((3072, 4096, 5120, 6144 + 1024)):
                unit(s, 2 * u, w_in, c + i * COL)
        loop(sp, Chain(None), 4, 0, diff)

        def branch(j):
            s = At("branch", j - 1, 8, 6)
            for n in range(2):
                c = j * (2 * COL) + (n - 2) * COL
                unit(s, 4 * n, w_in, c + 8192)
                unit(s, 4 * n + 2, a["w_br_moba"][0], c, rows=1024)
                unit(s, 4 * n + 3, a["w_br_diff"][0], c, rows=1024)
        loop(sp, Chain(None), 5, 0, branch, start=1)

        def square(name, w):
            def body(i):
                s = At(name, i, 4, 2)
                for u in range(2):
                    unit(s, 2 * u, w, i * (2 * COL) + u * COL)
            loop(sp, Chain(None), 4, 0, body)

        square("out1", a["w_out"][0])

        def ffn1(b):
            def up(i):
                s = At("ffn1", i, 4, 2, outer_turn=b * 8, outer_units=b * 16)
                for u in range(2):
                    unit(s, 2 * u, a["w_up"][0], b * 2048 + i * 512 + u * COL)

            def down(i):
                s = At("ffn1", i, 4, 2, g=16, u=8, outer_turn=b * 8, outer_units=b * 16)
                for u in range(2):
                    unit(s, 2 * u, a["w_down"][0], i * 512 + u * COL, row0=b * 2048)
            loop(sp, Chain(None), 4, 0, up)
            loop(sp, Chain(None), 4, 0, down)
        loop(sp, Chain(None), 4, 0, ffn1)

        def proj(name, w):
            for g in range(2):
                load(At(name), g, w[:, g * 1024:g * 1024 + 1024])
        proj("proj1", a["w_ple_proj"][0])
        square("gate1", a["w_ple_gate"][0])


        w_in_q2 = w_in2

        def mlstm(i):
            s = At("mlstm", i, 8, 4)
            for u, c in enumerate((0, 1024, 2048, 3072)):
                unit(s, 2 * u, w_in_q2, c + i * COL)
        loop(sp, Chain(None), 4, 0, mlstm)

        def fox(i):
            s = At("fox", i, 12, 6)
            for q in range(2):
                for u, c in enumerate((4104, 5128, 6152)):
                    unit(s, 6 * q + 2 * u, w_in_q2, c + q * COL + i * (2 * COL))
        loop(sp, Chain(None), 2, 0, fox)
        square("out2", a["w_out_2"][0])

        def ffn2(name, b, pairs, rows):
            turn, units = (b * 12, b * 24) if name == "ffn2" else (0, 0)
            col0 = b * 2048 if name == "ffn2" else 4096

            def up(i):
                s = At(name, i, 4, 2, outer_turn=turn, outer_units=units)
                unit(s, 0, a["w_up_2"][0], col0 + i * COL)
                unit(s, 2, a["w_up_2"][0], FF2 + col0 + i * COL)

            def down(i):
                s = At(name, i, 4, 2, g=4 * pairs, u=2 * pairs, outer_turn=turn, outer_units=units)
                for u in range(2):
                    unit(s, 2 * u, a["w_down_2"][0], i * 512 + u * COL, row0=col0, rows=rows)
            loop(sp, Chain(None), pairs, 0, up)
            loop(sp, Chain(None), 4, 0, down)
        loop(sp, Chain(None), 2, 0, lambda b: ffn2("ffn2", b, 8, 2048))
        ffn2("ffn2b", 0, 6, 1536)
        proj("proj2", a["w_ple_proj_2"][0])
        square("gate2", a["w_ple_gate_2"][0])
        for k in range(4):
            sp.wait_ge(out_copied, 2 * k + 2)
            sp.dma_start(out[0, (k // 2) * P:(k // 2) * P + P, (k % 2) * 1024:(k % 2) * 1024 + 1024],
                         out_rows[:, k // 2, (k % 2) * 1024:(k % 2) * 1024 + 1024]).then_inc(out_landed, 16)
        sp.wait_ge(out_landed, 64)

    @block.gpsimd
    def _(pool):
        for k, n in enumerate(vectors1):
            pool.dma_start(vec_rows[16 * k:16 * k + 16, 0, :], a[n][0].rearrange("(k c) -> k c", c=P)).then_inc(vec_landed if k else gain_landed, 16)
        for n in vectors2:
            r0, nr = col[n] - P, a[n].shape[-1] // P
            pool.dma_start(vec_rows[r0:r0 + nr, 1, :], a[n][0].rearrange("(k c) -> k c", c=P)).then_inc(vec_landed, 16)
        for w in range(4):
            src = a["conv_w_2"][0, w] if w < 3 else a["conv_b_2"][0]
            r0 = FFT2 * (w % 2)
            pool.dma_start(vec_rows[r0:r0 + FFT2, 2 + w // 2, :], src.rearrange("(k c) -> k c", c=P)).then_inc(vec_landed, 16)

        steps = Chain(pool_steps)

        def rope(p):
            pool.wait_ge(rot_done, p + 1)
            nc.gpsimd.tensor_tensor(QK[0:32], QK[0:32], over(rope_cos, 4), ALU.mult).then_inc(rope_cos_done, 1)

        rope(0)
        loop(pool, steps, 8, 0, rope, start=1)

        def clear_acc():
            steps.step(nc.gpsimd.memset(acc[:, :, :], 0.0))
            pool.wait_ge(pool_steps, steps.done())

        def sum_units(k0, written, base, tile_of, sq=sq):
            def body(i):
                for u in range(2):
                    pool.wait_ge(written, base + 2 * i + u + 1)
                    src = tile_of(i, u)
                    steps.step(nc.gpsimd.tensor_tensor(sq[:, :, :], src, src, ALU.mult))
                    pool.wait_ge(pool_steps, steps.done())
                    nc.gpsimd.tensor_tensor(acc[:, :, :], acc[:, :, :], sq[:, :, :], ALU.add).then_inc(unit_squares, 1)
                    pool.wait_ge(unit_squares, k0 + 2 * i + u + 1)
            loop(pool, steps, 4, 2, body)

        def g_tile(i, u):
            return G[:, bass.ds(4 * i + 2 * u, 2), :]

        def h_tile(i, u):
            return h[:, bass.ds(4 * i + 2 * u, 2), :]

        pool.wait_ge(gated, 8)
        clear_acc()
        sum_units(0, evac_done, U0["out1"], g_tile)
        pool.wait_ge(o_ready, 12)
        pool.dma_start(emb[:, :, :], a["p"][0, 0].rearrange("(a p) d -> p a d", p=P)).then_inc(p_landed, 16)
        pool.wait_ge(x1_ready, 12)
        pool.wait_ge(sums_done, 3)
        nc.gpsimd.memset(G[:, :, :], 0.0).then_inc(tiles_done, 1)
        clear_acc()
        sum_units(8, tiles_done, TILES_FFN1 + 24, g_tile)
        pool.wait_ge(sums_done, 4)
        clear_acc()
        sum_units(16, gated, 8, g_tile, sq=sq_gate)
        pool.wait_ge(gated, 16)
        w_in2 = a["w_in_2"][0]
        for c0, n, src in ((0, 4, 4100), (4, 8, 7176), (12, 4, 4096)):
            pool.dma_start(gate_w[:, :, c0:c0 + n], w_in2[:, src:src + n].rearrange("(k p) c -> p k c", p=P)).then_inc(gate_w_landed, 16)
        gb = a["mlstm_gate_bias_2"][0]
        for r0, n, src in ((0, 4, gb[4:8]), (4, 8, a["fox_f_bias_2"][0]), (12, 4, gb[0:4])):
            pool.dma_start(small[r0:r0 + n, 40:41], src.rearrange("(k c) -> k c", c=1)).then_inc(gate_w_landed, 16)


        def wt(i):
            pool.wait_ge(gates, GATE_STEPS)
            if not isinstance(i, int):
                pool.wait_ge(pt_gated, i)
            row = G_MAX[:, bass.ds(i, 1), :].rearrange("p a t -> p (a t)")
            steps.step(nc.gpsimd.tensor_tensor(PR[:, 0, 0:TOK], mask_t[:, 0:TOK], row, ALU.subtract))
            row1 = G_MAX[:, bass.ds(i, 1), P:TOK].rearrange("p a t -> p (a t)")
            nc.gpsimd.tensor_tensor(PR[:, 0, TOK:384], mask_t[:, TOK:384], row1, ALU.subtract).then_inc(wt_arg, 1)
        wt(0)
        loop(pool, steps, 4, 1, wt, start=1)

        pool.wait_ge(o_ready, 16)

        def decay(q):
            pool.wait_ge(logits_done, 16 + 2 * q)
            for hh in range(2):
                rows = G_DECAY[:, bass.ds(2 * q + hh, 1), :].rearrange("p a t -> p (a t)")
                first = G_DECAY[:, bass.ds(2 * q + hh, 1), 0:P].rearrange("p a t -> p (a t)")
                steps.step(nc.gpsimd.tensor_tensor(DK[:, hh, 0:P], mask[:, 0:P], first, ALU.add))
                nc.gpsimd.tensor_tensor(DK[:, hh, P:384], mask[:, P:384], rows, ALU.add).then_inc(bias_done, 1)
        loop(pool, steps, 4, 2, decay)

        pool.wait_ge(evac_done, U0["out2"])
        clear_acc()
        sum_units(24, tiles_done, TILES_OUT2, h_tile)
        pool.wait_ge(o_ready, 24)
        pool.dma_start(emb[:, :, :], a["p_2"][0, 0].rearrange("(a p) d -> p a d", p=P)).then_inc(p_landed, 16)
        pool.wait_ge(sums_done, 8)
        clear_acc()
        sum_units(32, tiles_done, TILES_FFN2 + 16, h_tile)

    @block.scalar
    def _(act):
        steps = Chain(act_steps)
        A = nc.scalar.activation

        def hi(at, m):
            k = 2 * at.g + m + LEAD
            act.wait_ge(raw_landed[(k // 2) % RING], 16 * (k // 2 // RING + 1) + 16 * at.turn)
            if not (isinstance(at.turn, int) and k + 8 * at.turn < RING):
                act.wait_ge(half_used, k - RING + 1 + 8 * at.turn)
            A(split[:, k % RING, :, 0, :], raw[:, (k // 2) % RING, HALF * (k % 2):HALF * (k % 2) + HALF, :], ACT.Copy).then_inc(hi_done, 1)

        def evac(at, m, u):
            s = (at.u + u) % 2
            act.wait_ge(half_used, at.halves(m) + 1)
            A(cross[:, s], ps[:, 2 * s:2 * s + 2, TOK:512], ACT.Copy).then_inc(cross_done, 1)

        def each_half(at, rows, after, final=False):
            for m, (u, _, _, _, _, _, last) in enumerate(rows):
                if not (final and m + LEAD >= len(rows)):
                    hi(at, m)
                if last:
                    evac(at, m, u)
                after(m)

        def root(k, bank, scale=1.0 / DM):
            act.wait_ge(sums_done, k + 1)
            A(rn[:, 0, :], pw[:, bank, 0:TOK], ACT.Sqrt, bias=eps_col, scale=scale).then_inc(root_done, 1)

        def gained_hi(e, c, gain):
            for k in range(4):
                kt = 4 * c + k
                ins = A(X1[:, bass.ds(kt, 1), 0, :], h[:, bass.ds(kt, 1), :], ACT.Copy, scale=vec(gain, kt))
            ins.then_inc(x1_hi, 1)

        def gained_and_square_chunks(k, e, gain, hooks=None):
            for c in range(4):
                act.wait_ge(h_ready, 4 * k + c + 1)
                gained_hi(e, c, gain)
                A(G[:, 4 * c:4 * c + 4, :], h[:, 4 * c:4 * c + 4, :], ACT.Square).then_inc(squares_ready, 1)
                if hooks:
                    hooks[c]()

        act.wait_ge(eps_ready, 1)
        act.wait_ge(vec_turned, 1)
        A(cols[:, 0:16], pw[:, 3, 0:16], ACT.Copy).then_inc(vec_copied, 1)
        for c in range(4):
            act.wait_ge(x_turned, 2 * c + 2)
            A(h[:, 4 * c:4 * c + 4, :].rearrange("p (a b) t -> p a (b t)", a=2), pw[:, 2 * (c % 2):2 * (c % 2) + 2, :], ACT.Copy).then_inc(h_ready, 1)
            act.wait_ge(h_ready, c + 1)
            gained_hi(0, c, "g_mix_pre")
            if c < LEAD:
                hi(At("moba"), c - LEAD)

        def rn_column(n):
            act.wait_ge(rn_turned, n + 1)
            for q in range(2):
                ins = A(rn_col[:, q:q + 1], pw[:, 1, q * P:q * P + 1], ACT.Copy)
            ins.then_inc(rn_col_done, 1)

        def set_up_steps(m):
            if m == 0:
                for c in range(4):
                    A(G[:, 4 * c:4 * c + 4, :], h[:, 4 * c:4 * c + 4, :], ACT.Square).then_inc(squares_ready, 1)
            if m == 1:
                act.wait_ge(vec_turned, 2)
                A(cols[:, 16:P + n_rows2], pw[:, 0, 16:P + n_rows2], ACT.Copy).then_inc(vec_copied, 1)
                A(cols[:, P + 32:], pw[:, 1, 0:4 * FFT2], ACT.Copy).then_inc(vec_copied, 1)
            if m == 2:
                root(0, 0)
                act.wait_ge(lam_summed, 1)
                A(small[:, 22:24], pw[:, 1, 0:2], ACT.Exp).then_inc(lam_exps, 1)
            if m == 3:
                rn_column(0)

        def softmax_exps(k, heads=2):
            for hh in range(heads):
                act.wait_ge(logits_done, k + hh + 1)
                A(PR[:, hh, 0:P], PR[:, hh, 0:P], ACT.Exp, bias=small[:, 2 * hh:2 * hh + 1], scale=-1.0,
                  accum_out=small[:, 4 + 2 * hh:5 + 2 * hh])
                A(PR[:, hh, P:384], PR[:, hh, P:384], ACT.Exp, bias=small[:, 2 * hh + 1:2 * hh + 2], scale=-1.0,
                  accum_out=small[:, 5 + 2 * hh:6 + 2 * hh]).then_inc(exp_done, 1)

        def copy_pt(k, heads):
            for hh in range(heads):
                act.wait_ge(probs_turned, k + hh + 1)
                A(PT[:, hh, :], pw[:, hh, 0:384], ACT.Copy).then_inc(pt_ready, 1)

        def o_heads(k, tile):
            for hh in range(2):
                act.wait_ge(pv_done, k + hh + 1)
                A(X2[:, bass.ds(tile + hh, 1), 0, :], pw[:, 2 + hh, 0:TOK].unsqueeze(1), ACT.Copy).then_inc(o_hi, 1)

        def o_square(n):
            act.wait_ge(o_raw, n + 1)
            A(MX[:, 2:4, :], MX[:, 0:2, :], ACT.Square).then_inc(o_squares, 1)

        def o_norm(n):
            act.wait_ge(o_sums, n + 1)
            A(rn[:, 0, :], pw[:, 1, 0:TOK], ACT.Sqrt, bias=eps_col, scale=1.0 / 256).then_inc(o_root, 1)

        def o_pair(k, n, tile):
            act.wait_ge(o_normed, n + 1)
            A(X2[:, bass.ds(tile, 2), 0, :], MX[:, 0:2, :], ACT.Copy).then_inc(o_hi, 1)

        def gate_a(at, p):
            act.wait_ge(evac_done, at.unit(3) + 1)
            A(G[:, bass.ds(2 * p, 2), :], t[:, 1], ACT.Sigmoid).then_inc(sig_done, 1)

        def moba(i):
            s = At("moba", i, 8, 4)

            def after(m):
                if isinstance(i, int):
                    set_up_steps(m)
                if m == 11:
                    softmax_exps(2 * i)
                if m == 13:
                    copy_pt(2 * i, 2)
                if m == 15:
                    o_heads(2 * i, 2 * i)
                    gate_a(s, i)
            each_half(s, MIX, after)
        moba(0)
        loop(act, steps, 4, 0, moba, start=1)

        def diff(i):
            s = At("diff", i, 8, 4)

            def after(m):
                if m == 11:
                    softmax_exps(2 * i + 8)
                if m == 13:
                    copy_pt(8 + i, 1)
                if m == 15:
                    o_square(i)
                    gate_a(s, i + 4)
                if m == 2 and not isinstance(i, int):
                    finish_diff(i - 1)
            each_half(s, MIX, after)

        def finish_diff(j):
            o_norm(j)
            o_pair(8 + j, j, 8 + 2 * j)
        diff(0)
        loop(act, steps, 4, 0, diff, start=1)

        def branch(i):
            s = At("branch", i, 8, 6)

            def after(m):
                if m == 2 and isinstance(i, int):
                    finish_diff(3)
                if m in (3, 11):
                    n = m // 8
                    act.wait_ge(evac_done, s.unit(3 * n) + 1)
                    if not (isinstance(i, int) and i + n == 0):
                        act.wait_ge(gated, 2 * i + n)
                    A(sg[:, :, :], t[:, (s.u + 3 * n) % 2], ACT.Sigmoid).then_inc(sig_done, 1)
            each_half(s, BRANCH, after)
        branch(0)
        loop(act, steps, 4, 0, branch, start=1)
        for c in range(4):
            act.wait_ge(gated, 8)
            A(X1[:, 4 * c:4 * c + 4, 0, :], G[:, 4 * c:4 * c + 4, :], ACT.Copy).then_inc(x1_hi, 1)

        def plain(name, rows, g=0, u=0, per=(4, 2), **outer):
            def body(i):
                each_half(At(name, i, *per, g=g, u=u, **outer), rows, lambda m: None)
            return body
        loop(act, steps, 4, 0, plain("out1", TWO))

        root(1, 0)
        gained_and_square_chunks(1, 2, "g_mlp_pre")

        def ffn1(b):
            first = isinstance(b, int)

            def up(i):
                s = At("ffn1", i, 4, 2, outer_turn=b * 8, outer_units=b * 16)

                def after(m):
                    if m == 2 and first and isinstance(i, int):
                        root(2, 0)
                    if m % 4 == 3:
                        u = m // 4
                        k = b * 8 + 2 * i + u
                        act.wait_ge(hid_done, k + 1)
                        A(X2[:, bass.ds(4 * i + 2 * u, 2), 0, :], t[:, (s.u + u) % 2], ACT.Copy).then_inc(hid_hi, 1)
                each_half(s, TWO, after)
            if first:
                up(0)
            loop(act, steps, 4, 0, up, start=int(first))
            loop(act, steps, 4, 0, plain("ffn1", DOWN, 16, 8, outer_turn=b * 8, outer_units=b * 16))
        ffn1(0)
        loop(act, steps, 4, 0, ffn1, start=1)

        def embed(k):
            act.wait_ge(p_turned, k + 1)
            A(X2[:, 0:2, 0, :], pw[:, 2, :].rearrange("p (a t) -> p a t", a=2), ACT.Copy).then_inc(p_hi, 1)

        def proj_granule(at, g, k):
            hi(at, 2 * g)
            for c in range(4):
                if c == 2:
                    hi(at, 2 * g + 1)
                if c < 3:
                    act.wait_ge(pair_used, 3 * k + c + 1)
                    s = (at.u + 4 * g + c) % 2
                    A(cross[:, s], ps[:, 2 * s:2 * s + 2, TOK:512], ACT.Copy).then_inc(cross_done, 1)
                else:
                    evac(at, 2 * g + 1, 4 * g + c)

        s = At("proj1")
        embed(0)
        proj_granule(s, 0, 0)
        root(3, 0)
        gained_and_square_chunks(2, 3, "g_ple_pre", [lambda: None, lambda: proj_granule(s, 1, 1), lambda: None, lambda: None])

        def gate(name, used, final=False):
            def body(i):
                s = At(name, i, 4, 2)

                def after(m):
                    if m == 2 and name == "gate1" and isinstance(i, int):
                        root(4, 0)
                    if m % 4 == 3:
                        u = m // 4
                        act.wait_ge(evac_done, s.unit(u) + 1)
                        act.wait_ge(gated, used + 2 * i + u)
                        A(sg[:, :, :], t[:, (s.u + u) % 2], ACT.Sigmoid).then_inc(sig_done, 1)
                each_half(s, TWO, after, final)
            return body
        gate("gate1", 8)(0)
        loop(act, steps, 4, 0, gate("gate1", 8), start=1)

        root(5, 0)
        gained_and_square_chunks(3, 4, "mix_norm_g_2")

        def gate_step(k, out_, in_, func, **more):
            act.wait_ge(gates, k - 1)
            A(out_, in_, func, **more).then_inc(gates, 1)
        act.wait_ge(gate_w_landed, 96)
        A(gate_split[:, :, 0, :], gate_w[:, :, :], ACT.Copy).then_inc(gate_split_hi, 1)
        def gate_steps(m):
            if m == 2:
                root(6, 0)
            if m == 3:
                rn_column(1)
            if m == 4:
                gate_step(2, GR[0:16, 0], pw[0:16, 0, TOK:512], ACT.Copy)
                gate_step(5, GR[0:16, 2], GR[0:16, 1], ACT.Abs)
                gate_step(6, GR[0:16, 2], GR[0:16, 2], ACT.Exp, scale=-1.0)
                gate_step(7, GR[0:16, 2], GR[0:16, 2], ACT.Ln, bias=1.0)
            if m == 6:
                gate_step(10, small[:, 0:32], pw[:, 1, 0:32], ACT.Copy)
            if m == 7:
                gate_step(12, GR[0:16, 4], pw[0:16, 2, 0:TOK], ACT.Copy)
            if m == 9:
                gate_step(23, GR[0:4, 3], GR[0:4, 2], ACT.Exp, scale=-1.0)
                gate_step(25, small[:, 48:56], pw[:, 0, 0:8], ACT.Copy)
            if m == 10:
                gate_step(27, G_MAX.rearrange("p (a b) t -> p a (b t)", a=2), pw[:, 0:2, :], ACT.Copy)
                gate_step(28, G_FLOOR.rearrange("p (a b) t -> p a (b t)", a=2), pw[:, 2:4, :], ACT.Copy)
            if m == 11:
                gate_step(30, G_DECAY.rearrange("p (a b) t -> p a (b t)", a=4), pw[:, :, :], ACT.Copy, scale=-1.0)

        def mlstm(i):
            s = At("mlstm", i, 8, 4)

            first = isinstance(i, int)

            def after(m):
                if first:
                    gate_steps(m)
                elif m == 2:
                    finish_mlstm(i - 1)
                if m == (12 if first else 5):
                    act.wait_ge(wt_arg, i + 1)
                    A(PR[:, 0, 0:TOK], PR[:, 0, 0:TOK], ACT.Exp, bias=small[:, bass.ds(48 + i, 1)])
                    A(PR[:, 0, TOK:384], PR[:, 0, TOK:384], ACT.Exp, bias=small[:, bass.ds(52 + i, 1)]).then_inc(wt_done, 1)
                if m == (14 if first else 13):
                    act.wait_ge(den_done, i + 1)
                    A(rn[:, 0, :], pw[:, 1, 0:TOK], ACT.Abs).then_inc(den_abs, 1)
                    o_square(i + 4)
                if m == 15:
                    act.wait_ge(evac_done, s.unit(3) + 1)
                    A(sg[:, :, :], t[:, (s.u + 3) % 2], ACT.Sigmoid).then_inc(sig_done, 1)
            each_half(s, MIX, after)

        def finish_mlstm(j):
            o_norm(j + 4)
            o_pair(12 + j, j + 4, 2 * j)
        mlstm(0)
        loop(act, steps, 4, 0, mlstm, start=1)

        def fox(i):
            s = At("fox", i, 12, 6)

            def square_qk(r):
                act.wait_ge(evac_done, s.unit(3 * r + 1) + 1)
                A(MX, QK, ACT.Square).then_inc(qk_squares, 1)

            def root_qk(q):
                act.wait_ge(qk_sums, q + 1)
                A(MX.rearrange("p (a b) t -> p a (b t)", a=2), pw[:, 0:2, :], ACT.Sqrt, bias=eps_col, scale=1.0 / P).then_inc(qk_root, 1)

            def after(m):
                r, q = m // 12, 2 * i + m // 12
                if m in (7, 19):
                    square_qk(r)
                if m == 9:
                    root_qk(q)
                if m == 12:
                    softmax_exps(16 + 4 * i)
                if m == 14:
                    copy_pt(12 + 4 * i, 2)
                if m == 16:
                    o_heads(16 + 4 * i, 8 + 4 * i)
                if m == 21:
                    root_qk(q)
                if m == 23:
                    softmax_exps(18 + 4 * i)
                if i == 0 and m == 2:
                    finish_mlstm(3)
                if i == 1:
                    finish_fox(0, m)
            each_half(s, FOX, after)

        def finish_fox(j, m):
            if m == 1:
                copy_pt(14 + 4 * j, 2)
            if m == 2:
                o_heads(18 + 4 * j, 10 + 4 * j)
        fox(0)
        fox(1)

        def gained_units(name, tiles, rows, e, gain, g=0, u=0):
            def body(i):
                def after(m):
                    if name == "out2" and isinstance(i, int):
                        finish_fox(1, m)
                    if m == 7:
                        act.wait_ge(tiles_done, tiles + 2 * i + 2)
                        gained_hi(e, i, gain)
                each_half(At(name, i, 4, 2, g=g, u=u), rows, after)
            return body
        out2 = gained_units("out2", TILES_OUT2, TWO, 5, "ffn_norm_g_2")
        out2(0)
        loop(act, steps, 4, 0, out2, start=1)

        def ffn2(name, b, pairs, k0):
            turn, units = (b * 12, b * 24) if name == "ffn2" else (0, 0)

            def up(i):
                s = At(name, i, 4, 2, outer_turn=turn, outer_units=units)

                def after(m):
                    if m == 2 and name == "ffn2" and b == 0 and isinstance(i, int):
                        root(7, 0)
                    if m == 5:
                        act.wait_ge(conv_done, k0 + i + 1)
                        for j in range(2):
                            bias = cols[:, bass.ds(CONV_BIAS + (b * 16 if name == "ffn2" else 32) + 2 * i + j, 1)]
                            ins = A(sg[:, j, :], t[:, s.u % 2, j, :], ACT.Gelu, bias=bias)
                        ins.then_inc(sig_done, 1)
                    if m == 7:
                        act.wait_ge(hid_done, 32 + k0 + i + 1)
                        A(X2[:, bass.ds(2 * i, 2), 0, :], t[:, (s.u + 1) % 2], ACT.Copy).then_inc(hid_hi, 1)
                each_half(s, TWO, after)
            first = name == "ffn2" and b == 0
            if first:
                up(0)
            loop(act, steps, pairs, 0, up, start=int(first))
            if name == "ffn2":
                loop(act, steps, 4, 0, plain(name, DOWN, 4 * pairs, 2 * pairs, outer_turn=turn, outer_units=units))
            else:
                loop(act, steps, 4, 0, gained_units(name, TILES_FFN2 + 16, DOWN3, 6, "ple_norm_g_2", 4 * pairs, 2 * pairs))
        ffn2("ffn2", 0, 8, 0)
        ffn2("ffn2", 1, 8, 8)
        ffn2("ffn2b", 0, 6, 16)

        s2 = At("proj2")
        embed(1)
        proj_granule(s2, 0, 2)
        root(8, 0)
        proj_granule(s2, 1, 3)

        loop(act, steps, 3, 0, gate("gate2", 16))
        gate("gate2", 16, final=True)(3)
        for k in range(8):
            act.wait_ge(out_turned, k + 1)
            A(out_rows[:, k // 4, (k % 4) * 512:(k % 4) * 512 + 512], pw[:, k % 4, :], ACT.Copy).then_inc(out_copied, 1)

    @block.vector
    def _(dve):
        steps = Chain(dve_steps)
        TT, STT = nc.vector.tensor_tensor, nc.vector.scalar_tensor_tensor

        def settled():
            dve.wait_ge(dve_steps, steps.done())

        def lo(at, m):
            k = 2 * at.g + m + LEAD
            dve.wait_ge(hi_done, k + 1 + 8 * at.turn)
            TT(split[:, k % RING, :, 1, :], raw[:, (k // 2) % RING, HALF * (k % 2):HALF * (k % 2) + HALF, :],
               split[:, k % RING, :, 0, :], ALU.subtract).then_inc(lo_done, 1)

        def evac(at, u, dst):
            s = (at.u + u) % 2
            dve.wait_ge(cross_done, at.unit(u) + 1)
            TT(dst, ps[:, 2 * s:2 * s + 2, 0:TOK], cross[:, s], ALU.add).then_inc(evac_done, 1)

        def evac_normed(at, u, dst, norm=rn[:, 1, :]):
            s = (at.u + u) % 2
            dve.wait_ge(cross_done, at.unit(u) + 1)
            steps.step(TT(dst, ps[:, 2 * s:2 * s + 2, 0:TOK], cross[:, s], ALU.add))
            settled()
            TT(dst, dst, over(norm, 2), ALU.mult).then_inc(evac_done, 1)

        def evac_values(at, u):
            s = (at.u + u) % 2
            dve.wait_ge(cross_done, at.unit(u) + 1)
            steps.step(TT(V, ps[:, 2 * s:2 * s + 2, 0:TOK], cross[:, s], ALU.add))
            settled()
            steps.step(nc.vector.tensor_scalar(V[:, 0, :], V[:, 0, :], rn_col[:, 0:1], None, ALU.mult))
            nc.vector.tensor_scalar(V[:, 1, :], V[:, 1, :], rn_col[:, 1:2], None, ALU.mult).then_inc(evac_done, 1)

        def gained_lo(e, c, gain):
            dve.wait_ge(x1_hi, 4 * e + c + 1)
            for k in range(4):
                kt = bass.ds(4 * c + k, 1)
                ins = STT(X1[:, kt, 1, :], h[:, kt, :], vec(gain, 4 * c + k), X1[:, kt, 0, :], ALU.mult, ALU.subtract)
            ins.then_inc(x1_ready, 1)

        def evaced(at, u):
            dve.wait_ge(evac_done, at.unit(u) + 1)

        def each_half(at, rows, after, final=False):
            for m in range(len(rows)):
                if not (final and m + LEAD >= len(rows)):
                    lo(at, m)
                after(m)

        def inverse_root(k, dst=rn[:, 1, :]):
            dve.wait_ge(root_done, k + 1)
            nc.vector.reciprocal(dst, rn[:, 0, :]).then_inc(rn_ready, 1)
            dve.wait_ge(rn_ready, k + 1)

        def post_norm(k, gain, hooks=None):
            for c in range(4):
                for kt in range(4 * c, 4 * c + 4):
                    steps.step(STT(G[:, kt, :], G[:, kt, :], vec(gain, kt), rn[:, 1, :], ALU.mult, ALU.mult))
                settled()
                TT(h[:, 4 * c:4 * c + 4, :], h[:, 4 * c:4 * c + 4, :], G[:, 4 * c:4 * c + 4, :], ALU.add).then_inc(h_ready, 1)
                if hooks:
                    hooks[c]()

        nc.vector.memset(eps_col, EPS).then_inc(eps_ready, 1)
        for c in range(4):
            gained_lo(0, c, "g_mix_pre")
            if c < LEAD:
                lo(At("moba"), c - LEAD)

        def set_up_steps(m):
            if m == 1:
                dve.wait_ge(vec_copied, 3)
                c = col["lambda_q1"]
                steps.step(TT(small[:, 20:21], cols[:, c:c + 1], cols[:, c + 1:c + 2], ALU.mult))
                TT(small[:, 21:22], cols[:, c + 2:c + 3], cols[:, c + 3:c + 4], ALU.mult).then_inc(lam_parts, 1)
                c = col["diff_subln_g"]
                steps.step(nc.vector.tensor_scalar(g_sub_scaled, cols[:, c:c + 2], 1.0 - LAMBDA_INIT, None, ALU.mult))
                c = col["fox_q_g_2"]
                steps.step(nc.vector.tensor_scalar(gq_scaled, cols[:, c:c + 1], SCALE, None, ALU.mult))
            if m == 2:
                inverse_root(0, mix_rn)
            if m == 4:
                dve.wait_ge(lam_exps, 1)
                steps.step(STT(neg_lambda, small[:, 23:24], -LAMBDA_INIT, small[:, 22:23], ALU.add, ALU.subtract))
                settled()
                dve.wait_ge(rn_col_done, 1)

        def rope(p):
            dve.wait_ge(rot_done, p + 1)
            steps.step(TT(MX[0:32], pw[0:32, 0:2, :].rearrange("p a (b t) -> p (a b) t", b=2), over(rope_sin, 4), ALU.mult))
            settled()
            dve.wait_ge(rope_cos_done, p + 1)
            TT(QK[0:32], QK[0:32], MX[0:32], ALU.add).then_inc(rope_done, 1)

        def logits(scores, k, tables, scale):
            for hh in range(2):
                dve.wait_ge(scores_done, scores + hh + 1)
                table = tables(hh)
                steps.step(nc.vector.memset(small[:, 16 + hh:17 + hh], 0.0))
                for q, (a0, a1) in enumerate(((0, P), (P, 384))):
                    ins = nc.vector.tensor_tensor_reduce(
                        out=PR[:, hh, a0:a1], in0=pw[:, 2 + hh, a0:a1], in1=table[:, a0:a1], scale=-scale, scalar=3e38,
                        op0=ALU.add, op1=ALU.min, accum_out=small[:, 2 * hh + q:2 * hh + q + 1])
                ins.then_inc(logits_done, 1)

        def normalise(k, kp):
            for hh in range(2):
                dve.wait_ge(exp_done, k + hh + 1)
                steps.step(nc.vector.reciprocal(small[:, 8 + 2 * hh:10 + 2 * hh], small[:, 4 + 2 * hh:6 + 2 * hh]))
                settled()
                nc.vector.tensor_scalar(PR[:, hh, 0:P], PR[:, hh, 0:P], small[:, 8 + 2 * hh:9 + 2 * hh], None, ALU.mult)
                nc.vector.tensor_scalar(PR[:, hh, P:384], PR[:, hh, P:384], small[:, 9 + 2 * hh:10 + 2 * hh], None, ALU.mult).then_inc(probs_ready, 1)

        def o_lo_heads(k, tile):
            for hh in range(2):
                dve.wait_ge(o_hi, k + hh + 1)
                TT(X2[:, bass.ds(tile + hh, 1), 1, :], pw[:, 2 + hh, 0:TOK].unsqueeze(1), X2[:, bass.ds(tile + hh, 1), 0, :], ALU.subtract).then_inc(o_ready, 1)

        def o_inverse_root(n):
            dve.wait_ge(o_root, n + 1)
            steps.step(nc.vector.reciprocal(rn[:, 1, :], rn[:, 0, :]))
            settled()

        def o_lo_pair(k, tile):
            dve.wait_ge(o_hi, k + 1)
            TT(X2[:, bass.ds(tile, 2), 1, :], MX[:, 0:2, :], X2[:, bass.ds(tile, 2), 0, :], ALU.subtract).then_inc(o_ready, 1)

        def mask_tables(hh):
            return mask

        def moba(i):
            s = At("moba", i, 8, 4)

            def after(m):
                if isinstance(i, int):
                    set_up_steps(m)
                if m == 3:
                    evac_normed(s, 0, QK[:, 0:2, :], mix_rn)
                if m == 7:
                    evac_normed(s, 1, QK[:, 2:4, :], mix_rn)
                if m == 9:
                    rope(i)
                if m == 11:
                    logits(2 * i, 2 * i, mask_tables, SCALE)
                    evac_values(s, 2)
                    normalise(2 * i, 2 * i)
                if m == 15:
                    evac_normed(s, 3, t[:, (s.u + 3) % 2], mix_rn)
                    o_lo_heads(2 * i, 2 * i)
                    dve.wait_ge(sig_done, i + 1)
            each_half(s, MIX, after)
        moba(0)
        loop(dve, steps, 4, 10, moba, start=1)

        def diff(i):
            s = At("diff", i, 8, 4)

            def combine():
                dve.wait_ge(exp_done, 2 * i + 10)
                steps.step(nc.vector.reciprocal(small[:, 8:12], small[:, 4:8]))
                settled()
                steps.step(nc.vector.tensor_scalar(small[:, 12:14], small[:, 10:12], neg_lambda, None, ALU.mult))
                steps.step(nc.vector.tensor_scalar(PR[:, 0, 0:P], PR[:, 0, 0:P], small[:, 8:9], None, ALU.mult))
                steps.step(nc.vector.tensor_scalar(PR[:, 0, P:384], PR[:, 0, P:384], small[:, 9:10], None, ALU.mult))
                settled()
                STT(PR[:, 0, 0:P], PR[:, 1, 0:P], small[:, 12:13], PR[:, 0, 0:P], ALU.mult, ALU.add)
                STT(PR[:, 0, P:384], PR[:, 1, P:384], small[:, 13:14], PR[:, 0, P:384], ALU.mult, ALU.add).then_inc(probs_ready, 1)

            def after(m):
                if m == 3:
                    evac_normed(s, 0, QK[:, 0:2, :], mix_rn)
                if m == 7:
                    evac_normed(s, 1, QK[:, 2:4, :], mix_rn)
                if m == 9:
                    rope(i + 4)
                if m == 11:
                    logits(2 * i + 8, 2 * i + 8, mask_tables, SCALE)
                    evac_values(s, 2)
                    combine()
                if m == 15:
                    dve.wait_ge(pv_done, 8 + i + 1)
                    nc.vector.tensor_copy(MX[:, 0:2, :], pw[:, 2:4, 0:TOK]).then_inc(o_raw, 1)
                    evac_normed(s, 3, t[:, (s.u + 3) % 2], mix_rn)
                if m == 2 and not isinstance(i, int):
                    finish_diff(i - 1)
            each_half(s, MIX, after)

        def finish_diff(n):
            o_inverse_root(n)
            for j in range(2):
                ins = STT(MX[:, j, :], MX[:, j, :], g_sub_scaled[:, j:j + 1], rn[:, 1, :], ALU.mult, ALU.mult)
            ins.then_inc(o_normed, 1)
            o_lo_pair(8 + n, 8 + 2 * n)
        diff(0)
        loop(dve, steps, 4, 13, diff, start=1)

        def branch(i):
            s = At("branch", i, 8, 6)

            def after(m):
                if m == 2 and isinstance(i, int):
                    finish_diff(3)
                n = m // 8
                s0 = (s.u + 3 * n) % 2
                pair = bass.ds(4 * i + 2 * n, 2)
                if m % 8 == 3:
                    evac_normed(s, 3 * n, t[:, s0], mix_rn)
                if m % 8 == 5:
                    evac(s, 3 * n + 1, t[:, 1 - s0])
                    evaced(s, 3 * n + 1)
                    steps.step(TT(G[:, pair, :], G[:, pair, :], t[:, 1 - s0], ALU.mult))
                if m % 8 == 7:
                    dve.wait_ge(sig_done, 8 + 2 * i + n + 1)
                    evac(s, 3 * n + 2, t[:, s0])
                    evaced(s, 3 * n + 2)
                    steps.step(TT(t[:, s0], t[:, s0], sg, ALU.mult))
                    settled()
                    TT(G[:, pair, :], G[:, pair, :], t[:, s0], ALU.add).then_inc(gated, 1)
                    dve.wait_ge(gated, 2 * i + n + 1)
            each_half(s, BRANCH, after)
        branch(0)
        loop(dve, steps, 4, 6, branch, start=1)
        for c in range(4):
            dve.wait_ge(x1_hi, 4 + c + 1)
            TT(X1[:, 4 * c:4 * c + 4, 1, :], G[:, 4 * c:4 * c + 4, :], X1[:, 4 * c:4 * c + 4, 0, :], ALU.subtract).then_inc(x1_ready, 1)

        def out1(i):
            s = At("out1", i, 4, 2)

            def after(m):
                if m % 4 == 3:
                    u = m // 4
                    evac(s, u, G[:, bass.ds(4 * i + 2 * u, 2), :])
            each_half(s, TWO, after)
        loop(dve, steps, 4, 0, out1)
        def lo_behind(e, gain, hooks=None):
            def hook(c):
                if c:
                    gained_lo(e, c - 1, gain)
                if hooks:
                    hooks[c]()
            return [lambda c=c: hook(c) for c in range(4)]
        inverse_root(1)
        post_norm(1, "g_mix_post", lo_behind(2, "g_mlp_pre"))
        gained_lo(2, 3, "g_mlp_pre")

        def ffn1(b):
            first = isinstance(b, int)

            def up(i):
                s = At("ffn1", i, 4, 2, outer_turn=b * 8, outer_units=b * 16)

                def after(m):
                    if m == 2 and first and isinstance(i, int):
                        inverse_root(2)
                    if m % 4 == 3:
                        u = m // 4
                        k = b * 8 + 2 * i + u
                        tile = t[:, (s.u + u) % 2]
                        evac_normed(s, u, tile)
                        evaced(s, u)
                        STT(tile, tile, 0.0, tile, ALU.max, ALU.mult).then_inc(hid_done, 1)
                        dve.wait_ge(hid_hi, k + 1)
                        TT(X2[:, bass.ds(4 * i + 2 * u, 2), 1, :], tile, X2[:, bass.ds(4 * i + 2 * u, 2), 0, :], ALU.subtract).then_inc(hid_ready, 1)
                each_half(s, TWO, after)

            def down(i):
                s = At("ffn1", i, 4, 2, g=16, u=8, outer_turn=b * 8, outer_units=b * 16)

                def after(m):
                    if m % 4 == 3:
                        u = m // 4
                        tile, pair = t[:, (s.u + u) % 2], bass.ds(4 * i + 2 * u, 2)
                        evac(s, u, tile)
                        evaced(s, u)
                        dve.wait_ge(tiles_done, TILES_FFN1 + b * 8 + 2 * i + u)
                        TT(G[:, pair, :], G[:, pair, :], tile, ALU.add).then_inc(tiles_done, 1)
                each_half(s, DOWN, after)
            if first:
                up(0)
            loop(dve, steps, 4, 2, up, start=int(first))
            loop(dve, steps, 4, 0, down)
        ffn1(0)
        loop(dve, steps, 4, 8, ffn1, start=1)

        def embed(k):
            dve.wait_ge(p_hi, k + 1)
            TT(X2[:, 0:2, 1, :], pw[:, 2, :].rearrange("p (a t) -> p a t", a=2), X2[:, 0:2, 0, :], ALU.subtract).then_inc(p_ready, 1)

        def proj_granule(at, g):
            for c in range(4):
                if c % 2 == 0:
                    lo(at, 2 * g + c // 2)
                u = 4 * g + c
                evac(at, u, E[:, 2 * u:2 * u + 2, :])

        s = At("proj1")
        embed(0)
        proj_granule(s, 0)
        inverse_root(3)
        post_norm(2, "g_mlp_post", lo_behind(3, "g_ple_pre", [lambda: None, lambda: proj_granule(s, 1), lambda: None, lambda: None]))
        gained_lo(3, 3, "g_ple_pre")

        def gate(name, sig, gated0, dst, final=False):
            def body(i):
                s = At(name, i, 4, 2)

                def after(m):
                    if m == 2 and name == "gate1" and isinstance(i, int):
                        inverse_root(4)
                    if m % 4 == 3:
                        u = m // 4
                        pair = bass.ds(4 * i + 2 * u, 2)
                        evac_normed(s, u, t[:, (s.u + u) % 2])
                        dve.wait_ge(sig_done, sig + 2 * i + u + 1)
                        if dst is G:
                            TT(G[:, pair, :], E[:, pair, :], sg, ALU.mult).then_inc(gated, 1)
                        else:
                            steps.step(TT(sg, E[:, pair, :], sg, ALU.mult))
                            settled()
                            TT(h[:, pair, :], h[:, pair, :], sg, ALU.add).then_inc(gated, 1)
                        dve.wait_ge(gated, gated0 + 2 * i + u + 1)
                each_half(s, TWO, after, final)
            return body
        gate("gate1", 16, 8, G)(0)
        loop(dve, steps, 4, 2, gate("gate1", 16, 8, G), start=1)
        inverse_root(5)
        post_norm(3, "g_ple_post", lo_behind(4, "mix_norm_g_2"))
        gained_lo(4, 3, "mix_norm_g_2")

        dve.wait_ge(gate_split_hi, 1)
        TT(gate_split[:, :, 1, :], gate_w[:, :, :], gate_split[:, :, 0, :], ALU.subtract).then_inc(gate_split_lo, 1)

        def gate_steps(m):
            if m == 2:
                inverse_root(6, mix_rn)
                steps.step(nc.vector.tensor_copy(SEL[0:16], ident[0:16, 0:16].unsqueeze(2).to_broadcast([16, 16, P])))
            if m == 4:
                dve.wait_ge(rn_col_done, 2)
                dve.wait_ge(gates, 2)
                TT(GR[0:16, 1], pw[0:16, 0, 0:TOK], GR[0:16, 0], ALU.add).then_inc(gates, 1)
                dve.wait_ge(gates, 3)
                steps.step(TT(GR[0:16, 1], GR[0:16, 1], mix_rn[0:16], ALU.mult))
                settled()
                nc.vector.tensor_scalar(GR[0:16, 1], GR[0:16, 1], small[0:16, 40:41], None, ALU.add).then_inc(gates, 1)
                dve.wait_ge(gates, 7)
                STT(GR[0:16, 3], GR[0:16, 1], 0.0, GR[0:16, 2], ALU.min, ALU.subtract).then_inc(gates, 1)
                for pad in pads:
                    steps.step(nc.vector.memset(pad[:, 0:P], 0.0))
            if m == 7:
                dve.wait_ge(gates, 12)
                TT(GR[0:4, 0], pw[0:4, 3, 0:TOK], GR[0:4, 4], ALU.subtract).then_inc(gates, 1)
                dve.wait_ge(gates, 13)
                steps.step(nc.vector.tensor_copy(pads[0][:, P:384], GR[0:4, 0]))
                settled()
                for k in range(8):
                    src, dst, back = pads[k % 2], pads[1 - k % 2], 1 << k
                    nc.vector.tensor_tensor(dst[:, P:384], src[:, P:384], src[:, P - back:384 - back], ALU.max).then_inc(gates, 1)
                    dve.wait_ge(gates, 14 + k)
                TT(GR[0:4, 2], GR[0:4, 4], pads[0][:, P:384], ALU.add).then_inc(gates, 1)
        pads = [GR[0:4, 5:8, :].rearrange("p a b -> p (a b)")[:, 384 * k:384 * k + 384] for k in range(2)]

        def mlstm(i):
            s = At("mlstm", i, 8, 4)
            first = isinstance(i, int)

            def after(m):
                if m == 2 and not first:
                    finish_mlstm(i - 1)
                if m == 3:
                    evac_normed(s, 0, QK[:, 0:2, :], mix_rn)
                if m == 7:
                    evac_normed(s, 1, QK[:, 2:4, :], mix_rn)
                if first:
                    gate_steps(m)
                if m == (13 if first else 9):
                    dve.wait_ge(wt_done, i + 1)
                    dve.wait_ge(scores_done, 17 + i)
                    STT(PT[:, 0, :], pw[:, 2, 0:384], MLSTM_SCALE, PR[:, 0, :], ALU.mult, ALU.mult).then_inc(pt_gated, 1)
                if m == 11:
                    evac_values(s, 2)
                if m == (14 if first else 13):
                    dve.wait_ge(den_abs, i + 1)
                    steps.step(TT(rn[:, 1, :].unsqueeze(1), rn[:, 0, :].unsqueeze(1), G_FLOOR[:, bass.ds(i, 1), :], ALU.max))
                    settled()
                    steps.step(nc.vector.reciprocal(rn[:, 1, :], rn[:, 1, :]))
                    settled()
                    dve.wait_ge(pv_done, 13 + i)
                    TT(MX[:, 0:2, :], pw[:, 2:4, 0:TOK], over(rn[:, 1, :], 2), ALU.mult).then_inc(o_raw, 1)
                if m == 15:
                    evac_normed(s, 3, t[:, (s.u + 3) % 2], mix_rn)
            each_half(s, MIX, after)

        def finish_mlstm(n):
            o_inverse_root(n + 4)
            for j in range(2):
                steps.step(STT(MX[:, j, :], MX[:, j, :], cols[:, bass.ds(col["mlstm_out_g_2"] + j + 2 * n, 1)], rn[:, 1, :], ALU.mult, ALU.mult))
            settled()
            dve.wait_ge(sig_done, 24 + n + 1)
            TT(MX[:, 0:2, :], MX[:, 0:2, :], sg, ALU.mult).then_inc(o_normed, 1)
            o_lo_pair(12 + n, 2 * n)
        mlstm(0)
        loop(dve, steps, 4, 10, mlstm, start=1)

        def fox(i):
            s = At("fox", i, 12, 6)

            def norm_qk(q):
                dve.wait_ge(qk_root, q + 1)
                steps.step(nc.vector.reciprocal(MX, MX))
                settled()
                steps.step(STT(QK[:, 0:2, :], QK[:, 0:2, :], gq_scaled, MX[:, 0:2, :], ALU.mult, ALU.mult))
                STT(QK[:, 2:4, :], QK[:, 2:4, :], vec("fox_k_g_2", 0), MX[:, 2:4, :], ALU.mult, ALU.mult).then_inc(qk_ready, 1)

            def decay_tables(q):
                def table(hh):
                    dve.wait_ge(bias_done, 2 * q + hh + 1)
                    return DK[:, hh]
                return table

            def after(m):
                r = m // 12
                q = 2 * i + r
                if m % 12 == 3:
                    evac_normed(s, 3 * r, QK[:, 0:2, :], mix_rn)
                if m % 12 == 7:
                    evac_normed(s, 3 * r + 1, QK[:, 2:4, :], mix_rn)
                if m % 12 == 9:
                    norm_qk(q)
                if m % 12 == 11:
                    evac_values(s, 3 * r + 2)
                if m in (12, 23):
                    k = i * 4 + (2 if m == 23 else 0)
                    logits(20 + k, 16 + k, decay_tables(i * 2 + (1 if m == 23 else 0)), 1.0)
                    normalise(16 + k, 12 + k)
                if m == 16:
                    o_lo_heads(16 + 4 * i, 8 + 4 * i)
                if m == 2:
                    finish_mlstm(3) if i == 0 else finish_fox(0)
            each_half(s, FOX, after)

        def finish_fox(j):
            o_lo_heads(18 + 4 * j, 10 + 4 * j)
        fox(0)
        fox(1)

        def add_h(name, tiles, rows, g=0, u=0, outer_tiles=0, operand=None, **outer):
            def body(i):
                s = At(name, i, 4, 2, g=g, u=u, **outer)

                def after(m):
                    if m == 2 and name == "out2" and isinstance(i, int):
                        finish_fox(1)
                    if m % 4 == 3:
                        uu = m // 4
                        tile, pair = t[:, (s.u + uu) % 2], bass.ds(4 * i + 2 * uu, 2)
                        evac(s, uu, tile)
                        evaced(s, uu)
                        dve.wait_ge(tiles_done, tiles + 2 * i + uu + outer_tiles)
                        TT(h[:, pair, :], h[:, pair, :], tile, ALU.add).then_inc(tiles_done, 1)
                    if m == 7 and operand:
                        gained_lo(operand[0], i, operand[1])
                each_half(s, rows, after)
            return body
        out2 = add_h("out2", TILES_OUT2, TWO, operand=(5, "ffn_norm_g_2"))
        out2(0)
        loop(dve, steps, 4, 0, out2, start=1)
        dve.wait_ge(tiles_done, TILES_OUT2 + 8)
        steps.step(nc.vector.memset(a_pad[:, :, 0:2], 0.0))

        def ffn2(name, b, pairs, k0):
            turn, units = (b * 12, b * 24) if name == "ffn2" else (0, 0)
            tile0 = b * 16 if name == "ffn2" else 32

            def up(i):
                s = At(name, i, 4, 2, outer_turn=turn, outer_units=units)

                def tap(w, j):
                    return cols[:, bass.ds(CONV + w * FFT2 + j + tile0 + 2 * i, 1)]

                def after(m):
                    if m == 2 and name == "ffn2" and b == 0 and isinstance(i, int):
                        inverse_root(7)
                    if m == 3:
                        evac_normed(s, 0, a_pad[:, :, 2:TOK + 2])
                        evaced(s, 0)
                        tile = t[:, s.u % 2]
                        for j in range(2):
                            steps.step(nc.vector.tensor_scalar(tile[:, j, :], a_pad[:, j, 0:TOK], tap(0, j), None, ALU.mult))
                        settled()
                        for j in range(2):
                            steps.step(STT(tile[:, j, :], a_pad[:, j, 1:TOK + 1], tap(1, j), tile[:, j, :], ALU.mult, ALU.add))
                        settled()
                        for j in range(2):
                            ins = STT(tile[:, j, :], a_pad[:, j, 2:TOK + 2], tap(2, j), tile[:, j, :], ALU.mult, ALU.add)
                        ins.then_inc(conv_done, 1)
                    if m == 7:
                        tile = t[:, (s.u + 1) % 2]
                        evac_normed(s, 1, tile)
                        evaced(s, 1)
                        dve.wait_ge(sig_done, 28 + k0 + i + 1)
                        TT(tile, tile, sg, ALU.mult).then_inc(hid_done, 1)
                        dve.wait_ge(hid_hi, 32 + k0 + i + 1)
                        TT(X2[:, bass.ds(2 * i, 2), 1, :], tile, X2[:, bass.ds(2 * i, 2), 0, :], ALU.subtract).then_inc(hid_ready, 1)
                each_half(s, TWO, after)
            first = name == "ffn2" and b == 0
            if first:
                up(0)
            loop(dve, steps, pairs, 6, up, start=int(first))
            last = name == "ffn2b"
            loop(dve, steps, 4, 0, add_h(name, TILES_FFN2, DOWN3 if last else DOWN, 4 * pairs, 2 * pairs, outer_tiles=16 if last else b * 8,
                                         operand=(6, "ple_norm_g_2") if last else None, outer_turn=turn, outer_units=units))
        ffn2("ffn2", 0, 8, 0)
        ffn2("ffn2", 1, 8, 8)
        ffn2("ffn2b", 0, 6, 16)
        dve.wait_ge(tiles_done, TILES_FFN2 + 24)

        s2 = At("proj2")
        embed(1)
        proj_granule(s2, 0)
        inverse_root(8)
        proj_granule(s2, 1)
        loop(dve, steps, 3, 4, gate("gate2", 50, 16, h))
        gate("gate2", 50, 16, h, final=True)(3)

    @block.tensor
    def _(pe):
        MM, T = nc.tensor.matmul, nc.tensor.transpose

        def unit_start(at, u):
            k = at.unit(u) - 1
            if not (isinstance(k, int) and k <= 0):
                pe.wait_ge(evac_done, k)

        def blocks(at, m, u, form, op, b0, tiles, first, last):
            slot = (2 * at.g + m) % RING
            s = (at.u + u) % 2
            for n, kt in enumerate(tiles):
                w = split[:, slot, b0 + n]
                start, stop = first and n == 0, last and n == len(tiles) - 1
                for j in range(2):
                    bank, js = 2 * s + j, slice(j * P, j * P + P)
                    if form == "features":
                        stay_hi, stay_lo, move = w[:, 0, js], w[:, 1, js], op[:, kt]
                    else:
                        stay_hi, stay_lo, move = op[:, kt, 0, js], op[:, kt, 1, js], w
                    MM(ps[:, bank, :], stay_hi, move, start=start, stop=False, skip_group_check=True)
                    ins = MM(ps[:, bank, 0:TOK], stay_lo, move[:, 0, :], start=False, stop=stop, skip_group_check=True)
            return ins

        def each_half(at, rows, ready=None, before=None):
            for m, (u, form, op, k0, per, first, last) in enumerate(rows):
                if before:
                    before(m)
                if first:
                    unit_start(at, u)
                if ready:
                    ready(m, u, k0)
                pe.wait_ge(lo_done, at.halves(m) + 1)
                blocks(at, m, u, form, op, 0, range(k0, k0 + per), first, last).then_inc(half_used, 1)

        def x1_is(e):
            def ready(m, u, k0):
                if u == 0:
                    pe.wait_ge(x1_ready, 4 * e + k0 // 4 + 1)
            return ready

        def sum_acc(k):
            pe.wait_ge(unit_squares, 8 * k + 8)
            MM(pw[:, 0, 0:TOK], ones, acc[:, 0, :], start=True, stop=False)
            MM(pw[:, 0, 0:TOK], ones, acc[:, 1, :], start=False, stop=True).then_inc(sums_done, 1)

        def sum_tiles(k):
            for kt in range(KT):
                if kt % 4 == 0:
                    pe.wait_ge(squares_ready, 4 * k + kt // 4 + 1)
                ins = MM(pw[:, 0, 0:TOK], ones, G[:, kt, :], start=kt == 0, stop=kt == KT - 1)
            ins.then_inc(sums_done, 1)

        pe.wait_ge(const_landed, 16)
        pe.wait_ge(gain_landed, 16)
        T(pw[:, 3, 0:16], vec_rows[0:16, 0, :], ident[0:16, 0:16]).then_inc(vec_turned, 1)
        pe.wait_ge(vec_copied, 1)
        pe.wait_ge(x_landed, 16)
        for b in range(8):
            if b >= 4 and b % 2 == 0:
                pe.wait_ge(h_ready, b // 2 - 1)
            for f in range(2):
                for q in range(2):
                    kt = 2 * b + f
                    ins = T(pw[:, b % 4, f * TOK + q * P:f * TOK + q * P + P], x_rows[:, q, kt * P:kt * P + P], ident)
            ins.then_inc(x_turned, 1)

        def turn_norm(n, k):
            pe.wait_ge(rn_ready, k + 1)
            for q in range(2):
                ins = T(pw[:, 1, q * P:q * P + P], mix_rn[:, q * P:q * P + P], ident)
            ins.then_inc(rn_turned, 1)

        def set_up_steps(m):
            if m == 2:
                pe.wait_ge(vec_landed, 16 * 20)
                pe.wait_ge(h_ready, 3)
                T(pw[:, 0, 0:P], vec_rows[:, 0, :], ident)
                T(pw[:, 0, P:P + n_rows2], vec_rows[0:n_rows2, 1, :], ident[0:n_rows2, 0:n_rows2])
                T(pw[:, 1, 0:2 * FFT2], vec_rows[0:2 * FFT2, 2, :], ident[0:2 * FFT2, 0:2 * FFT2])
                T(pw[:, 1, 2 * FFT2:4 * FFT2], vec_rows[0:2 * FFT2, 3, :], ident[0:2 * FFT2, 0:2 * FFT2]).then_inc(vec_turned, 1)
            if m == 3:
                pe.wait_ge(vec_copied, 3)
                sum_tiles(0)
                pe.wait_ge(lam_parts, 1)
                MM(pw[:, 1, 0:2], ones, small[:, 20:22], start=True, stop=True).then_inc(lam_summed, 1)
            if m == 4:
                pe.wait_ge(lam_exps, 1)
                turn_norm(0, 0)

        def rotate(at, p):
            pe.wait_ge(evac_done, at.unit(1) + 1)
            for c in range(2):
                ins = MM(pw[:, c, :], rot, QK[0:32, 2 * c:2 * c + 2, :], start=True, stop=True)
            ins.then_inc(rot_done, 1)

        def score(k):
            for hh in range(2):
                MM(pw[:, 2 + hh, 0:P], QK[:, hh, 0:P], QK[:, 2 + hh, 0:P], start=True, stop=True)
                MM(pw[:, 2 + hh, P:384], QK[:, hh, P:TOK], QK[:, 2 + hh, :], start=True, stop=True).then_inc(scores_done, 1)

        def turn_probs(k, heads):
            for hh in range(heads):
                pe.wait_ge(probs_ready, k + hh + 1)
                for b in range(3):
                    ins = T(pw[:, hh, b * P:b * P + P], PR[:, hh, b * P:b * P + P], ident)
                ins.then_inc(probs_turned, 1)

        def weigh(bank, values, pt):
            MM(pw[:, bank, 0:TOK], values(0), pt[:, 0:TOK], start=True, stop=False, skip_group_check=True)
            return MM(pw[:, bank, P:TOK], values(1), pt[:, TOK:384], start=False, stop=True, skip_group_check=True)

        def weigh_heads(at, u, k):
            pe.wait_ge(evac_done, at.unit(u) + 1)
            for hh in range(2):
                pe.wait_ge(pt_ready, k + hh + 1)
                weigh(2 + hh, lambda key, hh=hh: V[:, key, hh * P:hh * P + P], PT[:, hh]).then_inc(pv_done, 1)

        def weigh_tiles():
            for j in range(2):
                ins = weigh(2 + j, lambda key, j=j: V[:, key, j * P:j * P + P], PT[:, 0])
            ins.then_inc(pv_done, 1)

        def sum_o(n):
            pe.wait_ge(o_squares, n + 1)
            MM(pw[:, 1, 0:TOK], ones, MX[:, 2, :], start=True, stop=False)
            MM(pw[:, 1, 0:TOK], ones, MX[:, 3, :], start=False, stop=True).then_inc(o_sums, 1)

        def moba(i):
            s = At("moba", i, 8, 4)

            def before(m):
                if isinstance(i, int):
                    set_up_steps(m)
                if m == 9:
                    rotate(s, i)
                if m == 11:
                    pe.wait_ge(rope_done, i + 1)
                    if not isinstance(i, int):
                        pe.wait_ge(o_ready, 2 * i)
                    score(2 * i)
                if m == 13:
                    turn_probs(2 * i, 2)
                if m == 15:
                    weigh_heads(s, 2, 2 * i)
            each_half(s, MIX, x1_is(0), before)
        moba(0)
        loop(pe, Chain(None), 4, 0, moba, start=1)

        def diff(i):
            s = At("diff", i, 8, 4)

            def before(m):
                if m == 9:
                    pe.wait_ge(o_ready, 8 + i)
                    rotate(s, i + 4)
                if m == 11:
                    pe.wait_ge(rope_done, i + 5)
                    pe.wait_ge(o_ready, 8 + i)
                    score(2 * i + 8)
                if m == 13:
                    turn_probs(8 + i, 1)
                if m == 15:
                    pe.wait_ge(evac_done, s.unit(2) + 1)
                    pe.wait_ge(pt_ready, 8 + i + 1)
                    weigh_tiles()
                if m == 2 and not isinstance(i, int):
                    sum_o(i - 1)
            each_half(s, MIX, None, before)
        diff(0)
        loop(pe, Chain(None), 4, 0, diff, start=1)

        def finish_diff(m):
            if m == 2:
                sum_o(3)
            if m == 4:
                pe.wait_ge(o_ready, 12)
        each_half(At("branch"), BRANCH, None, finish_diff)
        loop(pe, Chain(None), 4, 0, lambda i: each_half(At("branch", i, 8, 6), BRANCH), start=1)
        loop(pe, Chain(None), 4, 0, lambda i: each_half(At("out1", i, 4, 2), TWO, x1_is(1)))
        sum_acc(0)

        def first_sums(k):
            def before(m):
                if m == 3:
                    sum_tiles(k)
            return before

        def ffn1(b):
            first = isinstance(b, int)
            outer = dict(outer_turn=b * 8, outer_units=b * 16)

            def hidden(m, u, k0):
                if u == 0:
                    pe.wait_ge(hid_ready, b * 8 + k0 // 2 + 2)
            if first:
                each_half(At("ffn1"), TWO, x1_is(2), first_sums(1))
            loop(pe, Chain(None), 4, 0, lambda i: each_half(At("ffn1", i, 4, 2, **outer), TWO, x1_is(2)), start=int(first))
            loop(pe, Chain(None), 4, 0, lambda i: each_half(At("ffn1", i, 4, 2, g=16, u=8, **outer), DOWN, hidden))
        ffn1(0)
        loop(pe, Chain(None), 4, 0, ffn1, start=1)

        def embed(k):
            pe.wait_ge(p_landed, 16 * (k + 1))
            for f in range(2):
                for q in range(2):
                    ins = T(pw[:, 2, f * TOK + q * P:f * TOK + q * P + P], emb[:, q, f * P:f * P + P], ident)
            ins.then_inc(p_turned, 1)

        def proj_granule(at, g):
            pe.wait_ge(lo_done, at.halves(2 * g) + 2)
            for c in range(4):
                u = 4 * g + c
                unit_start(at, u)
                first = blocks(at, 2 * g, u, "features", X2, c, range(1), True, False)
                last = blocks(at, 2 * g + 1, u, "features", X2, c, range(1, 2), False, True)
                if c < 3:
                    last.then_inc(pair_used, 1)
                else:
                    first.then_inc(half_used, 1)
                    last.then_inc(half_used, 1)

        s = At("proj1")
        embed(0)
        pe.wait_ge(p_ready, 1)
        proj_granule(s, 0)
        sum_acc(1)
        proj_granule(s, 1)
        each_half(At("gate1"), TWO, x1_is(3), first_sums(2))
        loop(pe, Chain(None), 4, 0, lambda i: each_half(At("gate1", i, 4, 2), TWO, x1_is(3)), start=1)
        sum_acc(2)

        def gate_steps(m):
            if m == 3:
                sum_tiles(3)
            if m == 4:
                turn_norm(1, 6)
                pe.wait_ge(gate_split_lo, 1)
                for kt in range(KT):
                    MM(pw[0:16, 0, :], gate_split[:, kt, 0, :], X1[:, kt], start=kt == 0, stop=False, skip_group_check=True)
                    ins = MM(pw[0:16, 0, 0:TOK], gate_split[:, kt, 1, :], X1[:, kt, 0, :], start=False, stop=kt == KT - 1, skip_group_check=True)
                ins.then_inc(gates, 1)
            if m == 7:
                pe.wait_ge(gates, 8)
                for q in range(2):
                    ins = T(pw[:, 1, 16 * q:16 * q + 16], GR[0:16, 3, q * P:q * P + P], ident[0:16, 0:16])
                ins.then_inc(gates, 1)
            if m == 8:
                pe.wait_ge(gates, 10)
                MM(pw[0:16, 2, 0:TOK], small[:, 0:16], tri, start=True, stop=False, skip_group_check=True)
                MM(pw[0:16, 2, P:TOK], small[:, 16:32], tri[:, 0:P], start=False, stop=True, skip_group_check=True)
                MM(pw[0:4, 3, 0:TOK], ident[0:16, 12:16], GR[0:16, 1], start=True, stop=True).then_inc(gates, 1)
            if m == 10:
                pe.wait_ge(gates, 23)
                for q in range(2):
                    ins = T(pw[:, 0, 4 * q:4 * q + 4], GR[0:4, 0, q * P:q * P + P], ident[0:4, 0:4])
                ins.then_inc(gates, 1)
            if m == 11:
                pe.wait_ge(gates, 25)
                top = GR[0:4, 5:8, :].rearrange("p a b -> p (a b)")[:, P:384]
                for r in range(4):
                    MM(pw[:, r // 2, (r % 2) * TOK:(r % 2) * TOK + TOK], SEL[0:4, r, :], top, start=True, stop=True)
                    ins = MM(pw[:, 2 + r // 2, (r % 2) * TOK:(r % 2) * TOK + TOK], SEL[0:4, r, :], GR[0:4, 3], start=True, stop=True)
                ins.then_inc(gates, 1)
            if m == 12:
                pe.wait_ge(gates, 28)
                for r in range(8):
                    ins = MM(pw[:, r // 2, (r % 2) * TOK:(r % 2) * TOK + TOK], SEL[0:16, 4 + r, :], GR[0:16, 4], start=True, stop=True)
                ins.then_inc(gates, 1)
            if m == 13:
                pe.wait_ge(gates, 30)

        def mlstm(i):
            s = At("mlstm", i, 8, 4)
            first = isinstance(i, int)

            def before(m):
                if first:
                    gate_steps(m)
                elif m == 2:
                    sum_o(i - 1 + 4)
                if m == (13 if first else 9):
                    pe.wait_ge(evac_done, s.unit(1) + 1)
                    pe.wait_ge(o_raw, i + 4)
                    for q, (a0, a1, t0) in enumerate(((0, TOK, 0), (TOK, 384, P))):
                        for c in range(2):
                            ins = MM(pw[:, 2, a0:a1], QK[:, 2 + c, q * P:q * P + P], QK[:, c, t0:TOK], start=c == 0, stop=c == 1)
                    ins.then_inc(scores_done, 1)
                if m == (15 if first else 13):
                    pe.wait_ge(pt_gated, i + 1)
                    pe.wait_ge(evac_done, s.unit(2) + 1)
                    weigh(1, lambda key: ones, PT[:, 0]).then_inc(den_done, 1)
                    weigh_tiles()
            each_half(s, MIX, x1_is(4), before)
        mlstm(0)
        loop(pe, Chain(None), 4, 0, mlstm, start=1)

        def fox(i):
            s = At("fox", i, 12, 6)

            def sum_qk(q):
                pe.wait_ge(qk_squares, q + 1)
                for c in range(2):
                    ins = MM(pw[:, c, :], ones, MX[:, 2 * c:2 * c + 2, :], start=True, stop=True)
                ins.then_inc(qk_sums, 1)

            def before(m):
                if m in (9, 21):
                    sum_qk(2 * i + m // 12)
                if m == 12:
                    pe.wait_ge(qk_ready, 2 * i + 1)
                    pe.wait_ge(o_ready, 16 + 4 * i)
                    score(20 + 4 * i)
                if m == 14:
                    turn_probs(12 + 4 * i, 2)
                if m == 16:
                    weigh_heads(s, 2, 12 + 4 * i)
                if m == 23:
                    pe.wait_ge(qk_ready, 2 * i + 2)
                    pe.wait_ge(o_ready, 18 + 4 * i)
                    score(22 + 4 * i)
                if i == 0 and m == 2:
                    sum_o(7)
                if i == 1:
                    finish_fox(s, 0, m)
            each_half(s, FOX, None, before)

        def finish_fox(at, j, m):
            if m == 1:
                turn_probs(14 + 4 * j, 2)
            if m == 2:
                weigh_heads(at, -1, 14 + 4 * j)
        fox(0)
        fox(1)

        def finish_last(m):
            finish_fox(At("out2"), 1, m)
            if m == 3:
                pe.wait_ge(o_ready, 24)
        each_half(At("out2"), OUT2, None, finish_last)
        loop(pe, Chain(None), 4, 0, lambda i: each_half(At("out2", i, 4, 2), OUT2), start=1)

        def ffn2(name, b, pairs, k0):
            outer = dict(outer_turn=b * 12, outer_units=b * 24) if name == "ffn2" else {}
            first = name == "ffn2" and b == 0

            def hidden(m, u, tile):
                if u == 0:
                    pe.wait_ge(hid_ready, 32 + k0 + min(tile // 2 + 2, pairs))
            if first:
                each_half(At(name), TWO, x1_is(5), lambda m: sum_acc(3) if m == 2 else None)
            loop(pe, Chain(None), pairs, 0, lambda i: each_half(At(name, i, 4, 2, **outer), TWO, x1_is(5)), start=int(first))
            loop(pe, Chain(None), 4, 0, lambda i: each_half(At(name, i, 4, 2, g=4 * pairs, u=2 * pairs, **outer), DOWN if name == "ffn2" else DOWN3, hidden))
        ffn2("ffn2", 0, 8, 0)
        ffn2("ffn2", 1, 8, 8)
        ffn2("ffn2b", 0, 6, 16)

        s2 = At("proj2")
        embed(1)
        pe.wait_ge(p_ready, 2)
        proj_granule(s2, 0)
        sum_acc(4)
        proj_granule(s2, 1)
        loop(pe, Chain(None), 4, 0, lambda i: each_half(At("gate2", i, 4, 2), TWO, x1_is(6)))
        pe.wait_ge(gated, 24)
        for k in range(8):
            if k >= 4:
                pe.wait_ge(out_copied, k - 3)
            for f in range(4):
                kt = 4 * (k % 4) + f
                ins = T(pw[:, k % 4, f * P:f * P + P], h[:, kt, (k // 4) * P:(k // 4) * P + P], ident)
            ins.then_inc(out_turned, 1)

    ctx.close()


def kernel(**inputs):
    import concourse.bacc as bacc
    from concourse.bass_utils import run_bass_kernel_spmd

    nc = bacc.Bacc("TRN2", target_bir_lowering=False, num_devices=1)
    arrays = {name: np.ascontiguousarray(inputs[name]) for name in INPUTS}
    arrays["constants"] = CONSTANTS
    aps = {n: nc.dram_tensor(f"in_{n}", v.shape, F32, kind="ExternalInput").ap() for n, v in arrays.items()}
    out = nc.dram_tensor("out", (1, TOK, DM), F32, kind="ExternalOutput").ap()
    two_blocks(nc, aps, out)
    r = run_bass_kernel_spmd(nc, [{f"in_{n}": v for n, v in arrays.items()}], core_ids=[0])
    return r.results[0]["out"]
```
